# Optimizing a Trainium2 kernel written in Bass

```python
import jax, jax.numpy as jnp
from jax import lax
import numpy as np

D_MODEL = 1024
BATCH = 1
SEQ = 2048
DEPTH = 2
DEC_BATCH = 8
DEC_SEQ = 1
PAST_LEN = 2048
PAGE_SIZE = 128

N_A = DEPTH // 2
N_B = DEPTH - N_A
N_HEADS = 16
HEAD_DIM = 64
N_KV = 2
GROUP = N_HEADS // N_KV
D_MAIN = N_HEADS * HEAD_DIM
D_RNN = D_MAIN
N_BLOCKS = 16
BLOCK_W = D_RNN // N_BLOCKS
CONV_W = 4
LRU_C = 8.0
WINDOW = 128
ROPE_THETA = 10000.0
N_MEM = 256
MEM_HEADS = 4
MEM_HD = 128
D_MEMW = MEM_HEADS * MEM_HD
D_IN = 2 * D_MAIN + 2 * D_MEMW
D_CAT = D_MAIN + D_MEMW
EPS = 1e-6
NEG = -1e30

kernel_name = "hawk_yoco_swa_sink_memxattn_step"

def rmsnorm(x, g):
    xf = x.astype(jnp.float32)
    y = xf * lax.rsqrt(jnp.mean(xf * xf, axis=-1, keepdims=True) + EPS)
    return (y * g.astype(jnp.float32)).astype(x.dtype)

def rope(x, pos):
    half = HEAD_DIM // 2
    inv = ROPE_THETA ** (-jnp.arange(half, dtype=jnp.float32) / half)
    ang = pos.astype(jnp.float32)[:, None] * inv[None, :]
    cos = jnp.cos(ang)[:, None, :]
    sin = jnp.sin(ang)[:, None, :]
    xf = x.astype(jnp.float32)
    x1, x2 = xf[..., :half], xf[..., half:]
    return jnp.concatenate([x1 * cos - x2 * sin, x2 * cos + x1 * sin], axis=-1).astype(x.dtype)

def causal_conv(u, buf, w, b):
    T = u.shape[1]
    up = jnp.concatenate([buf, u], axis=1)
    y = b + up[:, 0:T] * w[0]
    for k in range(1, CONV_W):
        y = y + up[:, k:k + T] * w[k]
    return y, up[:, T:]

def block_diag(u, w):
    ub = u.reshape(u.shape[:-1] + (N_BLOCKS, BLOCK_W))
    return jnp.einsum('btnc,ncd->btnd', ub, w).reshape(u.shape)

def rglru(u, h0, wa, ba, wx, bx, lam):
    f32 = jnp.float32
    uf = u.astype(f32)
    r = jax.nn.sigmoid(block_diag(uf, wa.astype(f32)) + ba.astype(f32))
    i = jax.nn.sigmoid(block_diag(uf, wx.astype(f32)) + bx.astype(f32))
    log_a = -LRU_C * r * jax.nn.softplus(-lam.astype(f32))
    a = jnp.exp(log_a)
    bterm = jnp.sqrt(-jnp.expm1(2.0 * log_a)) * (i * uf)

    def combine(c1, c2):
        a1, b1 = c1
        a2, b2 = c2
        return a1 * a2, a2 * b1 + b2

    acum, bcum = lax.associative_scan(combine, (a, bterm), axis=1)
    h = acum * h0.astype(f32)[:, None, :] + bcum
    return h.astype(u.dtype), h[:, -1].astype(u.dtype)

def mem_attend(q, mk, mv):
    s = jnp.einsum('bthd,bmhd->bhtm', q, mk, preferred_element_type=jnp.float32) * (MEM_HD ** -0.5)
    p = jax.nn.softmax(s, axis=-1).astype(mv.dtype)
    return jnp.einsum('bhtm,bmhd->bthd', p, mv)

def sink_attend(q, k, v, mask, sink):
    s = jnp.einsum('...qkgd,...skd->...kgqs', q, k, preferred_element_type=jnp.float32) * (HEAD_DIM ** -0.5)
    s = jnp.where(mask, s, NEG)
    sk = sink.astype(jnp.float32).reshape(N_KV, GROUP, 1, 1)
    m = jnp.maximum(jnp.max(s, axis=-1, keepdims=True), sk)
    p = jnp.exp(s - m)
    p = p / (jnp.sum(p, axis=-1, keepdims=True) + jnp.exp(sk - m))
    return jnp.einsum('...kgqs,...skd->...qkgd', p.astype(v.dtype), v)

def band_mask(nb):
    qi = jnp.arange(WINDOW)[:, None] + WINDOW
    ki = jnp.arange(2 * WINDOW)[None, :]
    local = (ki <= qi) & (qi - ki < WINDOW)
    valid = (jnp.arange(nb)[:, None, None] * WINDOW - WINDOW + ki[None]) >= 0
    return local[None] & valid

def shift_blocks(xb):
    return jnp.concatenate([jnp.zeros_like(xb[:, :1]), xb[:, :-1]], axis=1)

def trunk(x, pos, mem_k, mem_v, h0, conv0, win_k0, win_v0, prompt,
          norm_g, w_in, w_out, conv_w, conv_b, lru_wa, lru_ba, lru_wx, lru_bx, lru_lambda,
          kv_norm_g, w_kv, sinks, final_g):
    B, T, _ = x.shape
    new_h, new_conv = [], []
    for l in range(DEPTH):
        hn = rmsnorm(x, norm_g[l])
        proj = hn @ w_in[l]
        u, g_main, q_mem, g_mem = jnp.split(proj, [D_MAIN, 2 * D_MAIN, 2 * D_MAIN + D_MEMW], axis=-1)
        if l < N_A:
            uc, cbuf = causal_conv(u, conv0[l], conv_w[l], conv_b[l])
            y, h_last = rglru(uc, h0[l], lru_wa[l], lru_ba[l], lru_wx[l], lru_bx[l], lru_lambda[l])
            new_h.append(h_last)
            new_conv.append(cbuf)
        else:
            if l == N_A:
                kv = rmsnorm(x, kv_norm_g) @ w_kv
                k_new, v_new = jnp.split(kv, 2, axis=-1)
                k_new = rope(k_new.reshape(B, T, N_KV, HEAD_DIM), pos)
                v_new = v_new.reshape(B, T, N_KV, HEAD_DIM)
                if prompt:
                    nb = T // WINDOW
                    kb = k_new.reshape(B, nb, WINDOW, N_KV, HEAD_DIM)
                    vb = v_new.reshape(B, nb, WINDOW, N_KV, HEAD_DIM)
                    k_att = jnp.concatenate([shift_blocks(kb), kb], axis=2)
                    v_att = jnp.concatenate([shift_blocks(vb), vb], axis=2)
                    mask = band_mask(nb)[:, None, None]
                    win_k, win_v = k_new[:, T - WINDOW:], v_new[:, T - WINDOW:]
                else:
                    k_att = jnp.concatenate([win_k0, k_new], axis=1)
                    v_att = jnp.concatenate([win_v0, v_new], axis=1)
                    kpos = PAST_LEN - WINDOW + jnp.arange(WINDOW + T)
                    mask = (kpos[None, :] <= pos[:, None]) & (pos[:, None] - kpos[None, :] < WINDOW)
                    win_k, win_v = k_att[:, T:], v_att[:, T:]
            q = rope(u.reshape(B, T, N_HEADS, HEAD_DIM), pos)
            if prompt:
                q = q.reshape(B, T // WINDOW, WINDOW, N_KV, GROUP, HEAD_DIM)
            else:
                q = q.reshape(B, T, N_KV, GROUP, HEAD_DIM)
            y = sink_attend(q, k_att, v_att, mask, sinks[l - N_A]).reshape(B, T, D_MAIN)
        om = mem_attend(q_mem.reshape(B, T, MEM_HEADS, MEM_HD), mem_k[l], mem_v[l]).reshape(B, T, D_MEMW)
        z = jnp.concatenate([y * jax.nn.silu(g_main), om * jax.nn.silu(g_mem)], axis=-1)
        x = x + z @ w_out[l]
    return rmsnorm(x, final_g), jnp.stack(new_h), jnp.stack(new_conv), win_k, win_v

def setup_inputs(seed: int = 0) -> dict:
    key = jax.random.key(seed)
    ks = jax.random.split(key, 25)
    nrm = jax.random.normal
    a0 = jax.random.uniform(ks[20], (N_A, D_RNN), minval=0.9, maxval=0.999)
    return {
        'x_prompt': nrm(ks[0], (BATCH, SEQ, D_MODEL), jnp.float32),
        'x_sample': nrm(ks[1], (DEC_BATCH, DEC_SEQ, D_MODEL), jnp.float32),
        'cache_mem_k': nrm(ks[2], (DEPTH, DEC_BATCH, N_MEM, MEM_HEADS, MEM_HD), jnp.float32),
        'cache_mem_v': nrm(ks[3], (DEPTH, DEC_BATCH, N_MEM, MEM_HEADS, MEM_HD), jnp.float32),
        'state_lru_h': 0.5 * nrm(ks[4], (N_A, DEC_BATCH, D_RNN), jnp.float32),
        'state_conv': nrm(ks[5], (N_A, DEC_BATCH, CONV_W - 1, D_RNN), jnp.float32),
        'cache_win_k': nrm(ks[6], (DEC_BATCH, WINDOW, N_KV, HEAD_DIM), jnp.float32),
        'cache_win_v': nrm(ks[7], (DEC_BATCH, WINDOW, N_KV, HEAD_DIM), jnp.float32),
        'mem_prompt': nrm(ks[8], (BATCH, N_MEM, D_MODEL), jnp.float32),
        'norm_g': 1.0 + 0.05 * nrm(ks[9], (DEPTH, D_MODEL), jnp.float32),
        'w_in': nrm(ks[10], (DEPTH, D_MODEL, D_IN), jnp.float32) * D_MODEL ** -0.5,
        'w_out': nrm(ks[11], (DEPTH, D_CAT, D_MODEL), jnp.float32) * D_CAT ** -0.5,
        'mem_norm_g': 1.0 + 0.05 * nrm(ks[12], (DEPTH, D_MODEL), jnp.float32),
        'w_mem_kv': nrm(ks[13], (DEPTH, D_MODEL, 2 * D_MEMW), jnp.float32) * D_MODEL ** -0.5,
        'conv_w': nrm(ks[14], (N_A, CONV_W, D_RNN), jnp.float32) * CONV_W ** -0.5,
        'conv_b': 0.02 * nrm(ks[15], (N_A, D_RNN), jnp.float32),
        'lru_wa': nrm(ks[16], (N_A, N_BLOCKS, BLOCK_W, BLOCK_W), jnp.float32) * BLOCK_W ** -0.5,
        'lru_ba': 0.1 * nrm(ks[17], (N_A, D_RNN), jnp.float32),
        'lru_wx': nrm(ks[18], (N_A, N_BLOCKS, BLOCK_W, BLOCK_W), jnp.float32) * BLOCK_W ** -0.5,
        'lru_bx': 0.1 * nrm(ks[19], (N_A, D_RNN), jnp.float32),
        'lru_lambda': jnp.log(a0) - jnp.log1p(-a0),
        'kv_norm_g': 1.0 + 0.05 * nrm(ks[21], (D_MODEL,), jnp.float32),
        'w_kv': nrm(ks[22], (D_MODEL, 2 * N_KV * HEAD_DIM), jnp.float32) * D_MODEL ** -0.5,
        'sinks': 0.5 * nrm(ks[23], (N_B, N_HEADS), jnp.float32),
        'final_g': 1.0 + 0.05 * nrm(ks[24], (D_MODEL,), jnp.float32),
    }

def reference(x_prompt, x_sample, cache_mem_k, cache_mem_v, state_lru_h, state_conv,
              cache_win_k, cache_win_v, mem_prompt, norm_g, w_in, w_out, mem_norm_g, w_mem_kv,
              conv_w, conv_b, lru_wa, lru_ba, lru_wx, lru_bx, lru_lambda, kv_norm_g, w_kv,
              sinks, final_g):
    weights = (norm_g, w_in, w_out, conv_w, conv_b, lru_wa, lru_ba, lru_wx, lru_bx, lru_lambda,
               kv_norm_g, w_kv, sinks, final_g)
    mem_n = rmsnorm(mem_prompt[None], mem_norm_g[:, None, None, :])
    mkv = jnp.einsum('lbmd,lde->lbme', mem_n, w_mem_kv)
    mk_p, mv_p = jnp.split(mkv, 2, axis=-1)
    mk_p = mk_p.reshape(mk_p.shape[:3] + (MEM_HEADS, MEM_HD))
    mv_p = mv_p.reshape(mv_p.shape[:3] + (MEM_HEADS, MEM_HD))
    bp, tp = x_prompt.shape[0], x_prompt.shape[1]
    h0_p = jnp.zeros((N_A, bp, D_RNN), x_prompt.dtype)
    c0_p = jnp.zeros((N_A, bp, CONV_W - 1, D_RNN), x_prompt.dtype)
    pos_p = jnp.arange(tp, dtype=jnp.int32)
    y_p, h_p, conv_p, wk_p, wv_p = trunk(x_prompt, pos_p, mk_p, mv_p, h0_p, c0_p, None, None, True, *weights)
    pos_s = PAST_LEN + jnp.arange(x_sample.shape[1], dtype=jnp.int32)
    y_s, h_s, conv_s, wk_s, wv_s = trunk(x_sample, pos_s, cache_mem_k, cache_mem_v, state_lru_h, state_conv,
                                         cache_win_k, cache_win_v, False, *weights)
    return (y_p, y_s, mk_p, mv_p, h_p, conv_p, wk_p, wv_p, h_s, conv_s, wk_s, wv_s)


_drawn_inputs = setup_inputs


def setup_inputs(seed=0):
    import zlib

    import numpy as np

    out = dict(_drawn_inputs(seed))
    spreads = {}
    factors = {}
    for name, (base, spread) in spreads.items():
        noise = np.random.default_rng([zlib.crc32(name.encode()), seed]).standard_normal(out[name].shape)
        drawn = base * np.exp(spread * noise) if base else spread * noise
        out[name] = __import__('jax').numpy.asarray(drawn.astype(out[name].dtype))
    for name, factor in factors.items():
        out[name] = (out[name] * factor).astype(out[name].dtype)
    return out
```

```python
import numpy as np
import concourse.bass as bass
from concourse import mybir
from contextlib import ExitStack

F32 = mybir.dt.float32
F32R = mybir.dt.float32r
ALU = mybir.AluOpType
ACT = mybir.ActivationFunctionType
AX_X = mybir.AxisListType.X

D = 1024
KT = D // 128
T = 2048
TT = T // 128
NS = 8
TA = T + NS
CH = 512
NCH = T // CH
DIN = 3072
DMEM = 512
CAT = 1536
NI = CAT // 128
NMH = 4
M = 256
HD = 64
W = 128
NH = 16
EPS = 1e-6
NEG = -1e30
MEM_SCALE = 128 ** -0.5

R_CW, R_CB, R_BA, R_BX, R_LAM, R_G, R_KVG, R_MG, R_ST, R_H0, NR = 0, 4, 5, 6, 7, 8, 10, 11, 13, 37, 45


def ds(start, size):
    return slice(start, start + size) if isinstance(start, int) else bass.ds(start, size)


class Chain:

    def __init__(self, eng, sem, base=0):
        self.eng, self.sem, self.base, self.n = eng, sem, base, 0

    def link(self, ins):
        ins.then_inc(self.sem, 1)
        self.n += 1
        self.eng.wait_ge(self.sem, self.base + self.n)


class Mem:

    def __init__(self, nc, ctx):
        self.nc = nc
        base = 4224 + 32
        ctx.enter_context(nc.sbuf_tensor("fence", [128, (229344 - base) // 4], F32))
        self.HI = base
        self.WS = self.HI + KT * TA * 4
        self.LO = self.WS + 8 * KT * 128 * 4
        self.WK = self.LO + KT * TA * 4
        self.V0 = self.WK + 8192
        self.end = 229344

        def fixed(name, shape, dt=F32):
            place[0] += self.size(shape)
            return self.at(name, shape, place[0] - self.size(shape), dt)

        place = [self.WK]
        self.ident = fixed("ident", [128, 128])
        self.prm = fixed("prm", [128, KT, NR])
        self.dvp = fixed("dvp", [128, KT, 4])
        self.mask = fixed("mask", [128, 3, 128])
        self.sink_bc = fixed("sink_bc", [128, NH])
        self.sink_col = fixed("sink_col", [128, 1])
        self.eps = fixed("eps", [128, 1])
        self.stat = fixed("stat", [128, 64])
        self.bs = fixed("bs", [128, NI, NS])
        self.gth_s = fixed("gth_s", [128, NI, NS])
        self.gh_s = fixed("gh_s", [128, NI, NS])
        self.zs = fixed("zs", [128, NI, NS])
        self.out_t = fixed("out_t", [128, KT, 20])
        self.knew = fixed("knew", [128, 256])
        self.lru_par = fixed("lru_par", [128, 4])
        self.zs_hi = fixed("zs_hi", [128, NI, NS], F32R)
        self.zs_lo = fixed("zs_lo", [128, NI, NS], F32R)
        assert place[0] <= self.V0, place[0] - self.V0
        self.hn = self.at("hn", [128, KT, TA], self.LO)
        self.hn_hi = self.at("hn_hi", [128, KT, TA], self.HI, F32R)
        self.hn_lo = self.at("hn_lo", [128, KT, TA], self.LO, F32R)
        s = KT * 128 * 4
        self.w_raw = [[self.at(f"w_raw{p}{b}", [128, KT, 128], self.WS + (p * 4 + b * 2) * s) for b in range(2)] for p in range(2)]
        self.w_lo = [[self.at(f"w_lo{p}{b}", [128, KT, 128], self.WS + (p * 4 + b * 2) * s, F32R) for b in range(2)] for p in range(2)]
        self.w_hi = [[self.at(f"w_hi{p}{b}", [128, KT, 128], self.WS + (p * 4 + b * 2 + 1) * s, F32R) for b in range(2)] for p in range(2)]
        self.wo_hi = self.at("wo_hi", [128, NI, D], self.HI, F32R)
        self.wo_lo = self.at("wo_lo", [128, NI, D], self.HI + NI * D * 4, F32R)
        assert self.HI + 2 * NI * D * 4 <= self.LO
        self.kT = self.at("kT", [128, (TT + 1) * 128], self.V0 + 8192)
        self.kV = self.at("kV", [128, TT + 1, 128], self.V0 + 8192 + (TT + 1) * 512)
        self.kv_end = self.V0 + 8192 + 2 * (TT + 1) * 512
        self.bank = [ctx.enter_context(nc.psum_tensor(f"bank{i}", [128, 512], F32)) for i in range(8)]
        self.z_d = nc.dram_tensor("z_scratch", (NI, 128, T), F32).ap()
        self.x1_d = nc.dram_tensor("x1_scratch", (TA, D), F32).ap()
        self.kmt_d = nc.dram_tensor("kmt_scratch", (2, 128, NMH * M), F32).ap()

    @staticmethod
    def size(shape):
        return -(-int(np.prod(shape[1:])) * 4 // 32) * 32

    def at(self, name, shape, off, dt=F32):
        size = int(np.prod(shape[1:])) * 4
        assert off + size <= 229344, (name, off + size)
        return self.nc.alloc_sbuf_tensor_at(name, shape, dt, offset=off)


def bc(ap, n):
    return ap.unsqueeze(ap.ndim).broadcast_to(list(ap.shape) + [n])


def setup_phase(nc, m, sem, A):
    ld, ids, tr, ev = sem("su_ld"), sem("su_id"), sem("su_tr"), sem("su_ev")
    ch, ea, va = sem("su_ch"), sem("su_ea"), sem("su_va")
    rows = m.at("rows", [NR, D], m.V0)
    sp = m.at("sp", [128, 6, KT], m.V0 + 4096)
    ps = m.bank[0][:, :].rearrange("p (k r) -> p k r", k=KT)
    srcs = [(R_CW, 4, A["conv_w"][0]), (R_CB, 1, A["conv_b"]), (R_BA, 1, A["lru_ba"]), (R_BX, 1, A["lru_bx"]),
            (R_LAM, 1, A["lru_lambda"]), (R_G, 2, A["norm_g"]), (R_KVG, 1, A["kv_norm_g"].unsqueeze(0)),
            (R_MG, 2, A["mem_norm_g"]), (R_ST, 24, A["state_conv"][0].rearrange("b k d -> (b k) d")),
            (R_H0, 8, A["state_lru_h"][0])]
    nld = 16 * (len(srcs) + 1 + NS)
    with nc.Block() as block:
        @block.sync
        def _(sp_):
            for r, n, src in srcs:
                sp_.dma_start(rows[r:r + n, :], src).then_inc(ld, 16)
            sp_.dma_start(m.sink_bc[:, :], A["sinks"].broadcast_to([128, NH])).then_inc(ld, 16)
            for b in range(NS):
                sp_.dma_start(m.sink_col[b * NH:(b + 1) * NH, :], A["sinks"].rearrange("a h -> h a")).then_inc(ld, 16)
            sp_.wait_ge(ld, nld)

        @block.gpsimd
        def _(g):
            g.memset(m.ident[:, :], 0.0).then_inc(ids, 1)
            g.memset(m.mask[:, :, :], 0.0).then_inc(ids, 1)
            g.memset(m.eps[:, :], EPS).then_inc(ids, 1)
            g.wait_ge(ids, 3)
            g.affine_select(out=m.ident[:, :], in_=m.ident[:, :], compare_op=ALU.not_equal, fill=1.0,
                            base=0, pattern=[[-1, 128]], channel_multiplier=1).then_inc(ids, 1)
            g.memset(m.mask[:, 0, :], NEG).then_inc(ids, 1)
            g.affine_select(out=m.mask[:, 1, :], in_=m.mask[:, 1, :], compare_op=ALU.is_gt, fill=NEG,
                            base=0, pattern=[[1, 128]], channel_multiplier=-1).then_inc(ids, 1)
            g.affine_select(out=m.mask[:, 2, :], in_=m.mask[:, 2, :], compare_op=ALU.is_ge, fill=NEG,
                            base=0, pattern=[[-1, 128]], channel_multiplier=1).then_inc(ids, 1)
            g.wait_ge(ids, 7)

        @block.tensor
        def _(pe):
            pe.wait_ge(ld, nld)
            pe.wait_ge(ids, 4)
            for k in range(KT):
                last = nc.tensor.transpose(ps[:, k, 0:NR], rows[:, k * 128:(k + 1) * 128], m.ident[0:NR, 0:NR])
            last.then_inc(tr, 1)

        @block.scalar
        def _(act):
            act.wait_ge(ea, 2)
            nc.scalar.activation(sp[:, 1, :], sp[:, 0, :], ACT.Exp).then_inc(va, 1)

        @block.vector
        def _(v):
            c = Chain(v, ch)
            v.wait_ge(tr, 1)
            c.link(nc.vector.tensor_copy(m.prm[:, :, :], ps[:, :, 0:NR]))
            lam = m.prm[:, :, R_LAM]
            nc.vector.tensor_scalar(sp[:, 2, :], lam, -1.0, None, ALU.mult).then_inc(ea, 1)
            v.wait_ge(ea, 1)
            nc.vector.tensor_tensor(sp[:, 0, :], lam, sp[:, 2, :], ALU.min).then_inc(ea, 1)
            v.wait_ge(va, 1)
            c.link(nc.vector.tensor_scalar(sp[:, 3, :], sp[:, 1, :], 2.0, None, ALU.add))
            c.link(nc.vector.reciprocal(sp[:, 3, :], sp[:, 3, :]))
            c.link(nc.vector.tensor_tensor(sp[:, 3, :], sp[:, 3, :], sp[:, 1, :], ALU.mult))
            c.link(nc.vector.tensor_tensor(sp[:, 4, :], sp[:, 3, :], sp[:, 3, :], ALU.mult))
            c.link(nc.vector.tensor_scalar(sp[:, 5, :], sp[:, 4, :], 1.0 / 15, 1.0 / 13, ALU.mult, ALU.add))
            for q in (11, 9, 7, 5, 3, 1):
                c.link(nc.vector.tensor_tensor(sp[:, 5, :], sp[:, 5, :], sp[:, 4, :], ALU.mult))
                c.link(nc.vector.tensor_scalar(sp[:, 5, :], sp[:, 5, :], 1.0 / q, None, ALU.add))
            c.link(nc.vector.tensor_tensor(sp[:, 5, :], sp[:, 5, :], sp[:, 3, :], ALU.mult))
            c.link(nc.vector.tensor_scalar(sp[:, 2, :], sp[:, 2, :], 0.0, None, ALU.max))
            c.link(nc.vector.scalar_tensor_tensor(sp[:, 5, :], sp[:, 5, :], 2.0, sp[:, 2, :], ALU.mult, ALU.add))
            nc.vector.tensor_scalar(m.dvp[:, :, 0], sp[:, 5, :], -4.0, None, ALU.mult)
            nc.vector.tensor_scalar(m.dvp[:, :, 1], sp[:, 5, :], 4.0, None, ALU.mult)
            nc.vector.tensor_scalar(m.dvp[:, :, 2], m.prm[:, :, R_BA], 0.5, None, ALU.mult)
            nc.vector.tensor_scalar(m.dvp[:, :, 3], m.prm[:, :, R_BX], 0.5, None, ALU.mult)


def memory_phase(nc, m, sem, A, outs):
    ldx, ldw = sem("mm_ldx"), [sem(f"mm_ldw{i}") for i in range(4)]
    ss, x2, tr, hev, whi, wlo, hhi, hlo = (sem("mm_" + s) for s in ("ss", "x2", "tr", "hev", "whi", "wlo", "hhi", "hlo"))
    mmd, kvr, ktr, kte, st = (sem("mm_" + s) for s in ("mmd", "kvr", "ktr", "kte", "st"))
    ch = sem("mm_ch")
    V0 = m.V0
    x = m.at("mm_x", [128, 2, D], m.WS)
    junk = m.at("mm_junk", [128, D], m.WS + 8192)
    hnm = m.at("mm_hn", [128, KT, M], m.WS + 12288)
    hh = m.at("mm_hh", [128, KT, M], m.WS + 20480, F32R)
    hl = m.at("mm_hl", [128, KT, M], V0, F32R)
    stage = [m.at(f"mm_st{i}", [128, D], V0 + 8192 + 4096 * i) for i in range(4)]
    kv = [m.at(f"mm_kv{i}", [128, 2, D], V0 + 24576 + 8192 * i) for i in range(2)]
    ktb = [m.at(f"mm_kt{i}", [128, NMH, M], V0 + 40960 + 4096 * i) for i in range(2)]
    wh = m.at("mm_wh", [128, 2, KT, D], m.HI, F32R)
    wl = m.at("mm_wl", [128, 2, KT, D], m.LO, F32R)
    with nc.Block() as block:
        @block.sync
        def _(s):
            s.dma_start(x[:, :, :], A["mem_prompt"][0].rearrange("(t p) d -> p t d", p=128)).then_inc(ldx, 16)
            for q in range(2 * KT):
                l, k = q // KT, q % KT
                if q >= 4:
                    s.wait_ge(wlo, q - 3)
                s.dma_start(stage[q % 4][:, :], A["w_mem_kv"][l, k * 128:(k + 1) * 128, :]).then_inc(ldw[q % 4], 16)
            for l in range(2):
                for mt in range(2):
                    s.wait_ge(kvr, 2 * (2 * l + mt + 1))
                    for h, o in ((0, outs["mem_k"]), (1, outs["mem_v"])):
                        s.dma_start(o[l, 0].rearrange("m h d -> m (h d)")[mt * 128:(mt + 1) * 128, :],
                                    kv[l][:, mt, h * DMEM:(h + 1) * DMEM]).then_inc(st, 16)
            for l in range(2):
                s.wait_ge(kte, 2 * l + 2)
                s.dma_start(m.kmt_d[l], ktb[l][:, :, :].rearrange("p h m -> p (h m)")).then_inc(st, 16)
            s.wait_ge(st, 16 * 10)

        @block.scalar
        def _(act):
            act.wait_ge(ldx, 16)
            for t in range(2):
                nc.scalar.activation(junk[:, :], x[:, t, :], ACT.Square, accum_out=m.stat[:, t:t + 1]).then_inc(ss, 1)
                act.wait_ge(ss, t + 1)
            nc.scalar.activation(m.stat[:, 2:4], m.stat[:, 0:2], ACT.Sqrt, bias=m.eps[:, :], scale=1.0 / D).then_inc(ss, 1)
            for h in range(2):
                act.wait_ge(tr, h + 1)
                for t in range(2):
                    i = nc.scalar.activation(hnm[:, 4 * h:4 * h + 4, t * 128:(t + 1) * 128],
                                             m.bank[2 * h + t][:, :].rearrange("p (k c) -> p k c", k=4), ACT.Copy)
                i.then_inc(hev, 1)
            act.wait_ge(hev, 2)
            for q in range(2 * KT):
                l = q // KT
                if q % KT == 0:
                    for k in range(KT):
                        if q and k == 0:
                            act.wait_ge(mmd, 4)
                        nc.scalar.activation(hh[:, k, :], hnm[:, k, :], ACT.Copy, scale=m.prm[:, k, R_MG + l:R_MG + l + 1]).then_inc(hhi, 1)
                act.wait_ge(ldw[q % 4], 16 * (q // 4 + 1))
                nc.scalar.activation(wh[:, l, q % KT, :], stage[q % 4][:, :], ACT.Copy).then_inc(whi, 1)
            for i in range(4):
                act.wait_ge(ktr, i + 1)
                nc.scalar.activation(ktb[i // 2][:, 2 * (i % 2):2 * (i % 2) + 2, :],
                                     m.bank[6 + i % 2][:, :].rearrange("p (h c) -> p h c", h=2), ACT.Copy).then_inc(kte, 1)

        @block.vector
        def _(v):
            c = Chain(v, ch)
            v.wait_ge(ss, 3)
            c.link(nc.vector.reciprocal(m.stat[:, 4:6], m.stat[:, 2:4]))
            for t in range(2):
                nc.vector.tensor_scalar(x[:, t, :], x[:, t, :], m.stat[:, 4 + t:5 + t], None, ALU.mult).then_inc(x2, 1)

            def evac(i):
                l, mt, h = i // 4, i // 2 % 2, i % 2
                v.wait_ge(mmd, i + 1)
                nc.vector.tensor_copy(kv[l][:, mt, h * 512:(h + 1) * 512], m.bank[4 + i % 2][:, :]).then_inc(kvr, 1)

            v.wait_ge(hev, 2)
            for q in range(2 * KT):
                l, k = q // KT, q % KT
                if k == 0:
                    if l:
                        for i in range(4):
                            evac(i)
                    for k2 in range(KT):
                        v.wait_ge(hhi, l * KT + k2 + 1)
                        nc.vector.scalar_tensor_tensor(hl[:, k2, :], hnm[:, k2, :], m.prm[:, k2, R_MG + l:R_MG + l + 1],
                                                       hh[:, k2, :].bitcast(F32), ALU.mult, ALU.subtract).then_inc(hlo, 1)
                v.wait_ge(whi, q + 1)
                nc.vector.tensor_tensor(wl[:, l, k, :], stage[q % 4][:, :], wh[:, l, k, :].bitcast(F32), ALU.subtract).then_inc(wlo, 1)
            for i in range(4, 8):
                evac(i)

        @block.tensor
        def _(pe):
            for h in range(2):
                for t in range(2):
                    pe.wait_ge(x2, t + 1)
                    for k in range(4):
                        last = nc.tensor.transpose(m.bank[2 * h + t][:, k * 128:(k + 1) * 128],
                                                   x[:, t, (4 * h + k) * 128:(4 * h + k + 1) * 128], m.ident[:, :])
                last.then_inc(tr, 1)
            for i in range(8):
                l, mt, h = i // 4, i // 2 % 2, i % 2
                pe.wait_ge(hlo, KT * (l + 1))
                if i >= 2:
                    pe.wait_ge(kvr, i - 1)
                for k in range(KT):
                    pe.wait_ge(wlo, l * KT + k + 1)
                    a, b = hh[:, k, mt * 128:(mt + 1) * 128], hl[:, k, mt * 128:(mt + 1) * 128]
                    c, d = wh[:, l, k, h * 512:(h + 1) * 512], wl[:, l, k, h * 512:(h + 1) * 512]
                    for n, (p, q) in enumerate(((a, c), (a, d), (b, c))):
                        last = nc.tensor.matmul(m.bank[4 + i % 2][:, :], p, q, start=(k == 0 and n == 0), stop=(k == KT - 1 and n == 2))
                last.then_inc(mmd, 1)
            for i in range(4):
                l, hp = i // 2, i % 2
                pe.wait_ge(kvr, 4 * (l + 1))
                if i >= 2:
                    pe.wait_ge(kte, i - 1)
                for h in range(2):
                    for mt in range(2):
                        last = nc.tensor.transpose(m.bank[6 + i % 2][:, h * 256 + mt * 128:h * 256 + (mt + 1) * 128],
                                                   kv[l][:, mt, (2 * hp + h) * 128:(2 * hp + h + 1) * 128], m.ident[:, :])
                last.then_inc(ktr, 1)


def input_norm_phase(nc, m, sem, A):
    ldx = [sem(f"in_ldx{i}") for i in range(2)]
    ss, x2, tr, hev, ch = (sem("in_" + s) for s in ("ss", "x2", "tr", "hev", "ch"))
    V0 = m.V0
    x = [m.at(f"in_x{i}", [128, D], m.WS + 4096 * i) for i in range(2)]
    y = [m.at(f"in_y{i}", [128, D], m.WS + 8192 + 4096 * i) for i in range(2)]
    st = m.stat
    rows = lambda t: 128 if t < TT else NS
    with nc.Block() as block:
        @block.sync
        def _(s):
            for t in range(TT + 1):
                if t >= 2:
                    s.wait_ge(x2, t - 1)
                n = rows(t)
                src = A["x_prompt"][0, t * 128:(t + 1) * 128, :] if t < TT else A["x_sample"].rearrange("b s d -> (b s) d")
                s.dma_start(x[t % 2][0:n, :], src).then_inc(ldx[t % 2], 16)

        @block.scalar
        def _(act):
            for t in range(TT + 2):
                if t <= TT:
                    n, p = rows(t), t % 2
                    act.wait_ge(ldx[p], 16 * (t // 2 + 1))
                    if t >= 2:
                        act.wait_ge(tr, t - 1)
                    nc.scalar.activation(y[p][0:n, :], x[p][0:n, :], ACT.Square, accum_out=st[0:n, p:p + 1]).then_inc(ss, 1)
                    act.wait_ge(ss, 2 * t + 1)
                    nc.scalar.activation(st[0:n, 2 + p:3 + p], st[0:n, p:p + 1], ACT.Sqrt, bias=m.eps[0:n, :], scale=1.0 / D).then_inc(ss, 1)
                if t >= 1:
                    u, n = t - 1, rows(t - 1)
                    act.wait_ge(tr, u + 1)
                    for h in range(2):
                        i = nc.scalar.activation(m.hn[:, 4 * h:4 * h + 4, u * 128:u * 128 + n],
                                                 m.bank[2 * (u % 2) + h][:, :].rearrange("p (k c) -> p k c", k=4)[:, :, 0:n], ACT.Copy)
                    i.then_inc(hev, 1)

        @block.vector
        def _(v):
            c = Chain(v, ch)
            for t in range(TT + 1):
                n, p = rows(t), t % 2
                v.wait_ge(ss, 2 * t + 2)
                c.link(nc.vector.reciprocal(st[0:n, 4 + p:5 + p], st[0:n, 2 + p:3 + p]))
                nc.vector.tensor_scalar(y[p][0:n, :], x[p][0:n, :], st[0:n, 4 + p:5 + p], None, ALU.mult).then_inc(x2, 1)

        @block.tensor
        def _(pe):
            for t in range(TT + 1):
                n = rows(t)
                pe.wait_ge(x2, t + 1)
                if t >= 2:
                    pe.wait_ge(hev, t - 1)
                for k in range(KT):
                    last = nc.tensor.transpose(m.bank[2 * (t % 2) + k // 4][:, (k % 4) * 128:(k % 4) * 128 + n],
                                               y[t % 2][0:n, k * 128:(k + 1) * 128], m.ident[0:n, 0:n])
                last.then_inc(tr, 1)


def split_phase(nc, m, sem, l):
    hi = sem(f"sp_hi{l}")
    with nc.Block() as block:
        @block.scalar
        def _(act):
            for k in range(KT):
                nc.scalar.activation(m.hn_hi[:, k, :], m.hn[:, k, :], ACT.Copy, scale=m.prm[:, k, R_G + l:R_G + l + 1]).then_inc(hi, 1)

        @block.vector
        def _(v):
            for k in range(KT):
                v.wait_ge(hi, k + 1)
                nc.vector.scalar_tensor_tensor(m.hn_lo[:, k, :], m.hn[:, k, :], m.prm[:, k, R_G + l:R_G + l + 1],
                                               m.hn_hi[:, k, :].bitcast(F32), ALU.mult, ALU.subtract)


def item_phase(nc, m, sem, l, A):
    P = f"it{l}_"
    V0 = m.V0
    loaded = [sem(P + f"w_loaded{p}") for p in range(2)]
    names = ("w_hi w_lo b_done g_done b_free g_free kv_ld s_done m_ready e_done p_ready t_done pta_ready "
             "ptv_ready o_done z_ready gz_free mch chn ach swap cs_ld q_ready d_ready es_done uc_ready ri_done "
             "q2_ready sq_ready a_ready ip_ready").split()
    S = {n: sem(P + n) for n in names}
    stored = [sem(P + f"stored{p}") for p in range(2)]
    bd_ld = [sem(P + f"bd_ld{p}") for p in range(2)]
    PB, PG, S0, S1, S2, S3, T0, T1 = m.bank
    banks_s = [S0, S1, S2, S3]

    off = [V0]

    def buf(name, shape, dt=F32):
        t = m.at(P + name, shape, off[0], dt)
        off[0] += -(-int(np.prod(shape[1:])) * 4 // 32) * 32
        return t

    gth, gh = buf("gth", [128, CH]), buf("gh", [128, CH])
    gz = [buf(f"gz{i}", [128, CH]) for i in range(2)]
    if l == 0:
        start = off[0]
        u_sb = buf("u_sb", [128, 3 + T])
        uc = buf("uc", [128, CH])
        qT = m.at(P + "qT", [128, CH], start + 8224)
        thr, thi, tt_, m1, a2, q2 = (buf(n, [128, CH]) for n in ("thr", "thi", "tt", "m1", "a2", "q2"))
        aa = [buf(f"aa{i}", [128, CH]) for i in range(2)]
        hh = [buf(f"hh{i}", [128, CH]) for i in range(2)]
        bd = [[buf(f"bd{p}{g}", [128, 128]) for g in range(2)] for p in range(2)]
        Pm = m.at(P + "Pm", [128, 4, M], start)
        PTm = m.at(P + "PTm", [128, 2, CH], start + 4096)
        kmt, vm, vh = buf("kmt", [128, NMH, M]), buf("vm", [128, 2, DMEM]), buf("vh", [128, 2, 128])
    else:
        start = off[0]
        kT, kV = m.kT, m.kV
        off[0] = m.kv_end
        qraw, qrot, cs, qf = buf("qraw", [128, CH]), buf("qrot", [128, CH]), buf("cs", [128, 2, CH]), buf("qf", [128, CH])
        p0 = off[0]
        Ps = buf("Ps", [128, 2, 4, 2 * W])
        PTs = buf("PTs", [128, 2, 2, CH])
        sk = buf("sk", [128, 2])
        qT = m.at(P + "qT", [128, CH], m.kv_end)
        vh = m.at(P + "vh", [128, 2, 128], m.kv_end + 2048)
        Pm, kmt = m.at(P + "Pm", [128, 4, M], p0), m.at(P + "kmt", [128, NMH, M], p0 + 4096)
        PTm, vm = m.at(P + "PTm", [128, 2, CH], p0 + 8192), m.at(P + "vm", [128, 2, DMEM], p0 + 12288)
    dv_i = m.lru_par
    mx, negm, rs, rinv, es = (m.stat[:, 8 * i:8 * i + 8] for i in range(5))
    sden = m.stat[:, 40:48]
    w_in = A["w_in"][l].rearrange("(k p) n -> p k n", p=128)

    def cols(kind, j):
        if kind == "mem":
            return [[(2048 + 128 * j, 128, 0)], [(2560 + 128 * j, 128, 0)]]
        if l == 0:
            return [[(128 * j, 128, 0)], [(1024 + 128 * j, 128, 0)]]
        return [[(64 * j, 64, 0), (512 + 64 * j, 64, 64)], [(1024 + 64 * j, 64, 0), (1536 + 64 * j, 64, 64)]]

    main_inc = 32 if l == 0 else 64

    def load_w(s, kind, j, p):
        for b, pieces in enumerate(cols(kind, j)):
            for c0, n, o in pieces:
                s.dma_start(m.w_raw[p][b][:, :, o:o + n], w_in[:, :, ds(c0, n)]).then_inc(loaded[p], 16)
        if l == 0 and kind == "main":
            for g, w in enumerate(("lru_wa", "lru_wx")):
                for r in range(2):
                    s.dma_start(bd[p][g][64 * r:64 * r + 64, 64 * r:64 * r + 64],
                                A[w][0].rearrange("n c d -> (n c) d")[ds(128 * j + 64 * r, 64), :]).then_inc(bd_ld[p], 16)

    def loads_before(kind, i, p):
        return 32 * (i + 1) if kind == "mem" else 64 + main_inc * (i + 1)

    def split_act(act, kind, i, p):
        act.wait_ge(loaded[p], loads_before(kind, i, p))
        for b in range(2):
            nc.scalar.activation(m.w_hi[p][b][:, :, :], m.w_raw[p][b][:, :, :], ACT.Copy).then_inc(S["w_hi"], 1)

    def split_dve(v, kind, i, p):
        n = (0 if kind == "mem" else 4) + 2 * i + p
        for b in range(2):
            v.wait_ge(S["w_hi"], 2 * n + b + 1)
            nc.vector.tensor_tensor(m.w_lo[p][b][:, :, :], m.w_raw[p][b][:, :, :], m.w_hi[p][b][:, :, :].bitcast(F32),
                                    ALU.subtract).then_inc(S["w_lo"], 1)

    def next_item(kind, i, p, last):
        if p == 0:
            return kind, i, 1
        if not last:
            return kind, i + 1, 0
        return ("main", 0, 0) if kind == "mem" else None

    def project(pe, kind, i, p, b, c):
        n0 = (0 if kind == "mem" else 4) + p
        K = 10 * i + 5 * n0 + c
        ps = (PB, PG)[b]
        lo, w = (c * CH, CH) if c < NCH else (T, NS)
        pe.wait_ge(S["w_lo"], 4 * i + 2 * n0 + b + 1)
        pe.wait_ge(S["b_free" if b == 0 else "g_free"], K + 1)
        for k in range(KT):
            a, al = m.w_hi[p][b][:, k, :], m.w_lo[p][b][:, k, :]
            x, xl = m.hn_hi[:, k, lo:lo + w], m.hn_lo[:, k, lo:lo + w]
            for q, (s_, r_) in enumerate(((a, x), (a, xl), (al, x))):
                last = nc.tensor.matmul(ps[:, 0:w], s_, r_, start=(k == 0 and q == 0), stop=(k == KT - 1 and q == 2))
        last.then_inc(S["b_done" if b == 0 else "g_done"], 1)

    def evac_gate(act, kind, i, p, c):
        n0 = (0 if kind == "mem" else 4) + p
        K, n = 10 * i + 5 * n0 + c, 2 * i + n0
        act.wait_ge(S["g_done"], K + 1)
        if c < NCH:
            act.wait_ge(S["gz_free"], 8 * i + 4 * n0 + c + 1)
            a, b, w = gh[:, :], gth[:, :], CH
        else:
            a, b, w = m.gh_s[:, n, :], m.gth_s[:, n, :], NS
        nc.scalar.activation(a, PG[:, 0:w], ACT.Copy, scale=0.5)
        nc.scalar.activation(b, PG[:, 0:w], ACT.Tanh, scale=0.5).then_inc(S["g_free"], 1)

    def evac_branch(act, kind, i, p, c, dst):
        n0 = (0 if kind == "mem" else 4) + p
        act.wait_ge(S["b_done"], 10 * i + 5 * n0 + c + 1)
        w = CH if c < NCH else NS
        nc.scalar.activation(dst if c < NCH else m.bs[:, 2 * i + n0, :], PB[:, 0:w], ACT.Copy).then_inc(S["b_free"], 1)

    def gate_product(v, kind, i, p, c):
        n0 = (0 if kind == "mem" else 4) + p
        v.wait_ge(S["g_free"], 10 * i + 5 * n0 + c + 2)
        v.wait_ge(stored[c % 2], 64 * i + 32 * n0 + 16 * (c // 2) + 16)
        nc.vector.scalar_tensor_tensor(gz[c % 2][:, :], gth[:, :], 1.0, gh[:, :], ALU.add, ALU.mult).then_inc(S["gz_free"], 1)

    def store_z(s, kind, i, p, c):
        n0 = (0 if kind == "mem" else 4) + p
        s.wait_ge(S["z_ready"], 8 * i + 4 * n0 + c + 1)
        s.dma_start(m.z_d[ds(2 * i + n0, 1), :, c * CH:(c + 1) * CH].rearrange("a p t -> p (a t)"), gz[c % 2][:, :]).then_inc(stored[c % 2], 16)

    def mem_pe(pe, i, p):
        mb = 8 * i + 4 * p
        for c in range(NCH + 1):
            project(pe, "mem", i, p, 0, c)
            if c:
                pe.wait_ge(S["p_ready"], mb + c)
                for mt in range(2):
                    for t in range(4):
                        last = nc.tensor.transpose((T0, T1)[mt][:, t * 128:(t + 1) * 128], Pm[:, t, mt * 128:(mt + 1) * 128], m.ident[:, :])
                last.then_inc(S["t_done"], 1)
            project(pe, "mem", i, p, 1, c)
            if c:
                pe.wait_ge(S["pta_ready"], mb + c)
                pe.wait_ge(S["ptv_ready"], mb + c)
                for mt in range(2):
                    last = nc.tensor.matmul(S2[:, :], vh[:, mt, :], PTm[:, mt, :], start=(mt == 0), stop=(mt == 1))
                last.then_inc(S["o_done"], 1)
            if c < NCH:
                pe.wait_ge(S["kv_ld"], 32)
                pe.wait_ge(S["b_free"], 10 * i + 5 * p + c + 2)
                for t in range(4):
                    last = nc.tensor.matmul(banks_s[t // 2][:, (t % 2) * M:(t % 2 + 1) * M], qT[:, t * 128:(t + 1) * 128],
                                            kmt[:, ds(2 * i + p, 1), :].rearrange("q a k -> q (a k)"), start=True, stop=True)
                last.then_inc(S["s_done"], 1)

    def mem_act(act, i, p, last):
        mb = 8 * i + 4 * p
        for c in range(NCH + 1):
            if c:
                act.wait_ge(S["m_ready"], mb + c)
                for t in range(4):
                    nc.scalar.activation(Pm[:, t, :], banks_s[t // 2][:, (t % 2) * M:(t % 2 + 1) * M], ACT.Exp,
                                         bias=negm[:, t:t + 1], scale=MEM_SCALE, accum_out=rs[:, t:t + 1]).then_inc(S["e_done"], 1)
            evac_branch(act, "mem", i, p, c, qT[:, :])
            if c:
                act.wait_ge(S["t_done"], mb + c)
                nc.scalar.activation(PTm[:, 0, :], T0[:, :], ACT.Copy).then_inc(S["pta_ready"], 1)
            evac_gate(act, "mem", i, p, c)
            if c == 1 and next_item("mem", i, p, last):
                split_act(act, *next_item("mem", i, p, last))

    def mem_dve(v, i, p, last):
        mb = 8 * i + 4 * p
        chn = Chain(v, S["mch"], (2 * i + p) * 8)
        v.wait_ge(S["kv_ld"], 32)
        nc.vector.tensor_copy(vh[:, :, :], vm[:, :, ds((2 * i + p) * 128, 128)])
        for c in range(NCH + 1):
            if c:
                gate_product(v, "mem", i, p, c - 1)
                v.wait_ge(S["s_done"], mb + c)
                for b in range(2):
                    r = nc.vector.reduce_max(mx[:, 2 * b:2 * b + 2], banks_s[b][:, :].rearrange("p (t k) -> p t k", t=2), AX_X)
                chn.link(r)
                nc.vector.tensor_scalar(negm[:, 0:4], mx[:, 0:4], -MEM_SCALE, None, ALU.mult).then_inc(S["m_ready"], 1)
                v.wait_ge(S["e_done"], 4 * (mb + c))
                chn.link(nc.vector.reciprocal(rinv[:, 0:4], rs[:, 0:4]))
                for t in range(4):
                    r = nc.vector.tensor_scalar(Pm[:, t, :], Pm[:, t, :], rinv[:, t:t + 1], None, ALU.mult)
                r.then_inc(S["p_ready"], 1)
            if c == 1 and next_item("mem", i, p, last):
                split_dve(v, *next_item("mem", i, p, last))
            if c:
                v.wait_ge(S["t_done"], mb + c)
                nc.vector.tensor_copy(PTm[:, 1, :], T1[:, :]).then_inc(S["ptv_ready"], 1)
                v.wait_ge(S["o_done"], mb + c)
                v.wait_ge(S["gz_free"], mb + c + 1)
                g = gz[(c - 1) % 2]
                nc.vector.tensor_tensor(g[:, :], g[:, :], S2[:, :], ALU.mult).then_inc(S["z_ready"], 1)
        assert chn.n == 8

    def lru_pe(pe, i, p):
        mb = 8 * i + 4 * p
        for c in range(NCH + 1):
            project(pe, "main", i, p, 0, c)
            project(pe, "main", i, p, 1, c)
            if c < NCH:
                if c == 0:
                    pe.wait_ge(bd_ld[p], 64 * (i + 1))
                pe.wait_ge(S["uc_ready"], mb + c + 1)
                nc.tensor.matmul(S0[:, :], bd[p][0][:, :], uc[:, :], start=True, stop=True)
                nc.tensor.matmul(S1[:, :], bd[p][1][:, :], uc[:, :], start=True, stop=True).then_inc(S["ri_done"], 1)

    def lru_act(act, i, p, last):
        mb, f = 8 * i + 4 * p, 2 * i + p
        chn = Chain(act, S["ach"], (2 * i + p) * 5)
        chn.link(nc.scalar.activation(dv_i[:, :], m.dvp[:, ds(f, 1), :].rearrange("p a j -> p (a j)"), ACT.Copy))
        for c in range(NCH + 1):
            evac_branch(act, "main", i, p, c, u_sb[:, 3 + c * CH:3 + (c + 1) * CH] if c < NCH else None)
            if c:
                act.wait_ge(S["q2_ready"], mb + c)
                nc.scalar.activation(q2[:, :], q2[:, :], ACT.Sqrt, scale=0.25).then_inc(S["sq_ready"], 1)
            evac_gate(act, "main", i, p, c)
            if c == 1 and next_item("main", i, p, last):
                split_act(act, *next_item("main", i, p, last))
            if c < NCH:
                act.wait_ge(S["ri_done"], mb + c + 1)
                dv = lambda j: dv_i[:, j:j + 1]
                nc.scalar.activation(thi[:, :], S1[:, :], ACT.Tanh, bias=dv(3), scale=0.5)
                chn.link(nc.scalar.activation(thr[:, :], S0[:, :], ACT.Tanh, bias=dv(2), scale=0.5))
                nc.scalar.activation(aa[c % 2][:, :], thr[:, :], ACT.Exp, bias=dv(0), scale=dv(0))
                nc.scalar.activation(tt_[:, :], thr[:, :], ACT.Tanh, bias=dv(1), scale=dv(1)).then_inc(S["a_ready"], 1)
        assert chn.n == 5

    def lru_dve(v, i, p, last):
        mb, f, n0 = 8 * i + 4 * p, 2 * i + p, 4 + p
        CHN = 6 * NCH
        chn = Chain(v, S["chn"], (2 * i + p) * CHN)
        pr = lambda j: m.prm[:, ds(f, 1), j]
        for c in range(NCH + 1):
            if c < NCH:
                v.wait_ge(S["b_free"], 10 * i + 5 * n0 + c + 2)
                u = lambda k: u_sb[:, c * CH + k:c * CH + k + CH]
                chn.link(nc.vector.tensor_scalar(uc[:, :], u(0), pr(R_CW), pr(R_CB), ALU.mult, ALU.add))
                chn.link(nc.vector.scalar_tensor_tensor(uc[:, :], u(1), pr(R_CW + 1), uc[:, :], ALU.mult, ALU.add))
                chn.link(nc.vector.scalar_tensor_tensor(uc[:, :], u(2), pr(R_CW + 2), uc[:, :], ALU.mult, ALU.add))
                nc.vector.scalar_tensor_tensor(uc[:, :], u(3), pr(R_CW + 3), uc[:, :], ALU.mult, ALU.add).then_inc(S["uc_ready"], 1)
                if c == NCH - 1:
                    nc.vector.tensor_copy(m.out_t[:, ds(f, 1), 1:4].rearrange("p a k -> p (a k)"), u_sb[:, T:T + 3])
            if c:
                d = c - 1
                v.wait_ge(S["sq_ready"], mb + c)
                chn.link(nc.vector.tensor_tensor(m1[:, :], m1[:, :], q2[:, :], ALU.mult))
                init = 0.0 if d == 0 else hh[(d + 1) % 2][:, CH - 1:CH]
                chn.link(nc.vector.tensor_tensor_scan(hh[d % 2][:, :], aa[d % 2][:, :], m1[:, :], init, ALU.mult, ALU.add))
                gate_product(v, "main", i, p, d)
                v.wait_ge(S["gz_free"], 16 + mb + c + 1)
                g = gz[d % 2]
                nc.vector.tensor_tensor(g[:, :], g[:, :], hh[d % 2][:, :], ALU.mult).then_inc(S["z_ready"], 1)
                if d == NCH - 1:
                    nc.vector.tensor_copy(m.out_t[:, ds(f, 1), 0], hh[d % 2][:, CH - 1:CH])
            if c < NCH:
                v.wait_ge(S["a_ready"], mb + c + 1)
                v.wait_ge(S["uc_ready"], mb + c + 1)
                nc.vector.scalar_tensor_tensor(m1[:, :], thi[:, :], 1.0, uc[:, :], ALU.add, ALU.mult)
                chn.link(nc.vector.tensor_tensor(a2[:, :], aa[c % 2][:, :], aa[c % 2][:, :], ALU.mult))
                nc.vector.scalar_tensor_tensor(q2[:, :], a2[:, :], 1.0, tt_[:, :], ALU.add, ALU.mult).then_inc(S["q2_ready"], 1)
            if c == 1 and next_item("main", i, p, last):
                split_dve(v, *next_item("main", i, p, last))
        assert chn.n == CHN, chn.n

    def swa_pe(pe, i, p):
        mb = 8 * i + 4 * p
        for c in range(NCH + 1):
            project(pe, "main", i, p, 0, c)
            if c:
                pe.wait_ge(S["p_ready"], 16 + mb + c)
                for h in range(2):
                    for kt in range(2):
                        for t in range(4):
                            last = nc.tensor.transpose(((T0, T1), (S0, S1))[h][kt][:, t * 128:(t + 1) * 128],
                                                       Ps[:, h, t, kt * 128:(kt + 1) * 128], m.ident[:, :])
                last.then_inc(S["t_done"], 1)
            project(pe, "main", i, p, 1, c)
            if c:
                pe.wait_ge(S["pta_ready"], 16 + mb + c)
                pe.wait_ge(S["ptv_ready"], 16 + mb + c)
                for t in range(4):
                    for h in range(2):
                        for kt in range(2):
                            last = nc.tensor.matmul(T0[64 * h:64 * h + 64, t * 128:(t + 1) * 128],
                                                    kV[:, 4 * (c - 1) + t + kt, 64 * h:64 * h + 64],
                                                    PTs[:, h, kt, t * 128:(t + 1) * 128], start=(kt == 0), stop=(kt == 1))
                last.then_inc(S["o_done"], 1)
            if c < NCH:
                pe.wait_ge(S["q_ready"], mb + c + 1)
                for h in range(2):
                    for t in range(4):
                        last = nc.tensor.matmul(banks_s[2 * h + t // 2][:, (t % 2) * 256:(t % 2 + 1) * 256],
                                                qf[64 * h:64 * h + 64, t * 128:(t + 1) * 128],
                                                kT[64 * h:64 * h + 64, (4 * c + t) * 128:(4 * c + t + 2) * 128], start=True, stop=True)
                last.then_inc(S["s_done"], 1)

    def swa_act(act, i, p, last):
        mb = 8 * i + 4 * p
        for c in range(NCH + 1):
            if c:
                for h in range(2):
                    act.wait_ge(S["m_ready"], 16 + 2 * (mb + c - 1) + h + 1)
                    for t in range(4):
                        j = 4 * h + t
                        nc.scalar.activation(Ps[:, h, t, :], Ps[:, h, t, :], ACT.Exp, bias=negm[:, j:j + 1],
                                             accum_out=rs[:, j:j + 1]).then_inc(S["e_done"], 1)
                act.wait_ge(S["d_ready"], mb + c)
                nc.scalar.activation(es[:, :], es[:, :], ACT.Exp).then_inc(S["es_done"], 1)
            evac_branch(act, "main", i, p, c, qraw[:, :])
            if c:
                act.wait_ge(S["t_done"], 16 + mb + c)
                nc.scalar.activation(PTs[:, 0, 0, :], T0[:, :], ACT.Copy)
                nc.scalar.activation(PTs[:, 1, 0, :], S0[:, :], ACT.Copy).then_inc(S["pta_ready"], 1)
            evac_gate(act, "main", i, p, c)
            if c == 1 and next_item("main", i, p, last):
                split_act(act, *next_item("main", i, p, last))

    def swa_dve(v, i, p, last):
        mb, f, n0 = 8 * i + 4 * p, 2 * i + p, 4 + p
        CHN = 1 + 5 * NCH
        chn = Chain(v, S["chn"], f * CHN)
        nc.vector.tensor_copy(sk[:, 0:1], m.sink_bc[:, ds(f, 1)])
        chn.link(nc.vector.tensor_copy(sk[:, 1:2], m.sink_bc[:, ds(8 + f, 1)]))
        for c in range(NCH + 1):
            if c:
                v.wait_ge(S["s_done"], 16 + mb + c)
                gate_product(v, "main", i, p, c - 1)
                for h in range(2):
                    for t in range(4):
                        j = 4 * h + t
                        mk = m.mask[:, 0:3:2, :] if c == 1 and t == 0 else m.mask[:, 1:3, :]
                        sc = banks_s[2 * h + t // 2][:, (t % 2) * 256:(t % 2 + 1) * 256].rearrange("p (a k) -> p a k", a=2)
                        r = nc.vector.tensor_tensor_reduce(out=Ps[:, h, t, :].rearrange("p (a k) -> p a k", a=2), in0=sc, in1=mk, scale=1.0,
                                                           scalar=sk[:, h:h + 1], op0=ALU.add, op1=ALU.max, accum_out=mx[:, j:j + 1])
                    chn.link(r)
                    nc.vector.tensor_scalar(negm[:, 4 * h:4 * h + 4], mx[:, 4 * h:4 * h + 4], -1.0, None, ALU.mult).then_inc(S["m_ready"], 1)
                v.wait_ge(S["m_ready"], 16 + 2 * (mb + c))
                nc.vector.tensor_tensor(es[:, :].rearrange("p (h t) -> p h t", h=2), negm[:, :].rearrange("p (h t) -> p h t", h=2),
                                        bc(sk[:, :], 4), ALU.add).then_inc(S["d_ready"], 1)
                v.wait_ge(S["e_done"], 64 + 8 * (mb + c))
                v.wait_ge(S["es_done"], mb + c)
                chn.link(nc.vector.tensor_tensor(sden, rs[:, :], es[:, :], ALU.add))
                chn.link(nc.vector.reciprocal(rinv[:, :], sden))
                for j in range(8):
                    pj = Ps[:, j // 4, j % 4, :]
                    r = nc.vector.tensor_scalar(pj, pj, rinv[:, j:j + 1], None, ALU.mult)
                r.then_inc(S["p_ready"], 1)
            if c < NCH:
                v.wait_ge(S["swap"], 64 * (mb + c + 1))
                v.wait_ge(S["cs_ld"], 16 * (mb + c + 1))
                nc.vector.tensor_tensor(qraw[:, :], qraw[:, :], cs[:, 0, :], ALU.mult)
                chn.link(nc.vector.tensor_tensor(qrot[:, :], qrot[:, :], cs[:, 1, :], ALU.mult))
                nc.vector.tensor_tensor(qf[:, :], qraw[:, :], qrot[:, :], ALU.add).then_inc(S["q_ready"], 1)
            if c == 1 and next_item("main", i, p, last):
                split_dve(v, *next_item("main", i, p, last))
            if c:
                v.wait_ge(S["t_done"], 16 + mb + c)
                nc.vector.tensor_copy(PTs[:, 0, 1, :], T1[:, :])
                nc.vector.tensor_copy(PTs[:, 1, 1, :], S1[:, :]).then_inc(S["ptv_ready"], 1)
                v.wait_ge(S["o_done"], 16 + mb + c)
                v.wait_ge(S["gz_free"], 16 + mb + c + 1)
                g = gz[(c - 1) % 2]
                nc.vector.tensor_tensor(g[:, :], g[:, :], T0[:, :], ALU.mult).then_inc(S["z_ready"], 1)
        assert chn.n == CHN, chn.n

    def item_sp(s, kind, i, p, last):
        n0 = (0 if kind == "mem" else 4) + p
        nxt = next_item(kind, i, p, last)
        if nxt:
            if not (kind == "mem" and i == 0 and p == 0):
                s.wait_ge(S["g_done"], 10 * i + 5 * n0)
            load_w(s, nxt[0], 2 * nxt[1] + nxt[2], nxt[2])
        mb = 8 * i + 4 * p
        for c in range(NCH + 1):
            if l == 1 and kind == "main" and c < NCH:
                s.wait_ge(S["b_free"], 10 * i + 5 * n0 + c + 2)
                for r in range(4):
                    s.dma_start(qrot[32 * r:32 * r + 32, :], qraw[32 * (r ^ 1):32 * (r ^ 1) + 32, :]).then_inc(S["swap"], 16)
                s.dma_start(cs[:, :, :], A["rope_q"][:, :, c * CH:(c + 1) * CH]).then_inc(S["cs_ld"], 16)
            if c:
                store_z(s, kind, i, p, c - 1)

    main_pe = (lru_pe, swa_pe)[l]
    main_act = (lru_act, swa_act)[l]
    main_dve = (lru_dve, swa_dve)[l]
    NP = (NI - NMH) // 2

    def both(f, i, last=False):
        for p in range(2):
            f(i, p, last)

    def engine_loop(eng, mem_item, main_item):
        both(mem_item, 0)
        both(mem_item, 1, True)
        main_begin(eng)
        with eng.Fori(0, NP - 1) as i:
            both(main_item, i)
        both(main_item, NP - 1, True)

    def main_begin(eng):
        eng.wait_ge(S["o_done"], 16)
        if l == 0:
            eng.wait_ge(S["ip_ready"], 3)

    with nc.Block() as block:
        @block.sync
        def _(s):
            s.dma_start(kmt[:, :, :].rearrange("p h m -> p (h m)"), m.kmt_d[l]).then_inc(S["kv_ld"], 16)
            s.dma_start(vm[:, :, :], A["mem_v"][l, 0].rearrange("(t p) h d -> p t (h d)", p=128)).then_inc(S["kv_ld"], 16)
            for p in range(2):
                s.sem_inc(stored[p], 16)
            load_w(s, "mem", 0, 0)
            engine_loop(s, lambda i, p, last: item_sp(s, "mem", i, p, last), lambda i, p, last: item_sp(s, "main", i, p, last))
            for p in range(2):
                s.wait_ge(stored[p], 16 * (NI * NCH // 2 + 1))

        @block.gpsimd
        def _(g):
            if l == 0:
                for p in range(2):
                    for q in range(2):
                        for r in range(2):
                            last = g.memset(bd[p][q][64 * r:64 * r + 64, 64 * (1 - r):64 * (1 - r) + 64], 0.0)
                last.then_inc(S["ip_ready"], 1)
                g.wait_ge(S["ip_ready"], 1)
                g.wait_ge(S["o_done"], 16)
                g.memset(u_sb[:, 0:3], 0.0).then_inc(S["ip_ready"], 2)

        @block.scalar
        def _(act):
            act.sem_inc(S["b_free"], 1)
            act.sem_inc(S["g_free"], 1)
            split_act(act, "mem", 0, 0)
            engine_loop(act, lambda i, p, last: mem_act(act, i, p, last), lambda i, p, last: main_act(act, i, p, last))

        @block.vector
        def _(v):
            v.sem_inc(S["gz_free"], 1)
            split_dve(v, "mem", 0, 0)
            engine_loop(v, lambda i, p, last: mem_dve(v, i, p, last), lambda i, p, last: main_dve(v, i, p, last))

        @block.tensor
        def _(pe):
            engine_loop(pe, lambda i, p, last: mem_pe(pe, i, p), lambda i, p, last: main_pe(pe, i, p))


def sample_lru_phase(nc, m, sem, A, outs):
    ld, cp, ch, ga, mm, ex, sq, tr, ev, st = (sem("sl_" + s) for s in ("ld", "cp", "ch", "ga", "mm", "ex", "sq", "tr", "ev", "st"))
    zb = sem("sl_zb")
    H = m.HI
    n = KT * NS
    a = lambda name, k: m.at("sl_" + name, [128, KT, NS], H + 16384 + 256 * k)
    bd = m.at("sl_bd", [128, KT, 2, 128], H)
    uc, t1, thr, thi, ea, et, m1, a2, q2, h, gz = (a(s, k) for k, s in enumerate(("uc", "t1", "thr", "thi", "ea", "et", "m1", "a2", "q2", "h", "gz")))
    states = m.at("sl_rows", [20, D], H + 24576)
    R, I = (m.bank[b][:, 0:n].rearrange("p (k s) -> p k s", k=KT) for b in range(2))
    u = m.bs[:, NMH:NI, :]
    stt = m.prm[:, :, R_ST:R_ST + 24].rearrange("p k (s c) -> p k s c", c=3)
    col = lambda j: bc(m.prm[:, :, j], NS)
    dv = lambda j: bc(m.dvp[:, :, j], NS)
    with nc.Block() as block:
        @block.gpsimd
        def _(g):
            g.memset(bd[:, :, :, :], 0.0).then_inc(zb, 1)

        @block.sync
        def _(s):
            s.wait_ge(zb, 1)
            for q, w in enumerate(("lru_wa", "lru_wx")):
                for r in range(2):
                    s.dma_start(bd[64 * r:64 * r + 64, :, q, 64 * r:64 * r + 64],
                                A[w][0].rearrange("(k r) c d -> r c k d", r=2)[r]).then_inc(ld, 16)
            s.dma_start(outs["conv_s"][0, :, 0:2, :], A["state_conv"][0, :, 1:3, :]).then_inc(st, 16)
            s.wait_ge(ev, 1)
            s.dma_start(outs["lru_p"][0], states[0:1, :]).then_inc(st, 16)
            s.dma_start(outs["conv_p"][0, 0], states[1:4, :]).then_inc(st, 16)
            s.dma_start(outs["lru_s"][0], states[4:12, :]).then_inc(st, 16)
            s.dma_start(outs["conv_s"][0, :, 2, :], states[12:20, :]).then_inc(st, 16)
            s.wait_ge(st, 80)

        @block.tensor
        def _(pe):
            pe.wait_ge(ld, 64)
            pe.wait_ge(cp, 1)
            for k in range(KT):
                nc.tensor.matmul(R[:, k, :], bd[:, k, 0, :], uc[:, k, :], start=True, stop=True)
                last = nc.tensor.matmul(I[:, k, :], bd[:, k, 1, :], uc[:, k, :], start=True, stop=True)
            last.then_inc(mm, 1)
            pe.wait_ge(cp, 2)
            for k in range(KT):
                last = nc.tensor.transpose(m.bank[2 + k // 4][0:20, (k % 4) * 128:(k % 4 + 1) * 128], m.out_t[:, k, :], m.ident[:, :])
            last.then_inc(tr, 1)

        @block.scalar
        def _(act):
            act.wait_ge(ga, 2)
            nc.scalar.activation(thr[:, :, :], thr[:, :, :], ACT.Tanh, scale=0.5)
            nc.scalar.activation(thi[:, :, :], thi[:, :, :], ACT.Tanh, scale=0.5).then_inc(ex, 1)
            act.wait_ge(ga, 4)
            nc.scalar.activation(ea[:, :, :], ea[:, :, :], ACT.Exp)
            nc.scalar.activation(et[:, :, :], et[:, :, :], ACT.Tanh).then_inc(ex, 1)
            act.wait_ge(sq, 1)
            nc.scalar.activation(q2[:, :, :], q2[:, :, :], ACT.Sqrt, scale=0.25).then_inc(sq, 1)

        @block.vector
        def _(v):
            c = Chain(v, ch)
            tt = nc.vector.tensor_tensor
            c.link(tt(uc[:, :, :], u, col(R_CW + 3), ALU.mult))
            c.link(tt(uc[:, :, :], uc[:, :, :], col(R_CB), ALU.add))
            for k in range(3):
                c.link(tt(t1[:, :, :], stt[:, :, :, k], col(R_CW + k), ALU.mult))
                if k < 2:
                    c.link(tt(uc[:, :, :], uc[:, :, :], t1[:, :, :], ALU.add))
            tt(uc[:, :, :], uc[:, :, :], t1[:, :, :], ALU.add).then_inc(cp, 1)
            v.wait_ge(mm, 1)
            tt(thr[:, :, :], R, col(R_BA), ALU.add).then_inc(ga, 1)
            tt(thi[:, :, :], I, col(R_BX), ALU.add).then_inc(ga, 1)
            v.wait_ge(ex, 1)
            c.link(nc.vector.tensor_scalar(thr[:, :, :], thr[:, :, :], 1.0, None, ALU.add))
            tt(ea[:, :, :], thr[:, :, :], dv(0), ALU.mult).then_inc(ga, 1)
            tt(et[:, :, :], thr[:, :, :], dv(1), ALU.mult).then_inc(ga, 1)
            v.wait_ge(ex, 2)
            v.wait_ge(cp, 1)
            nc.vector.scalar_tensor_tensor(m1[:, :, :], thi[:, :, :], 1.0, uc[:, :, :], ALU.add, ALU.mult)
            c.link(tt(a2[:, :, :], ea[:, :, :], ea[:, :, :], ALU.mult))
            nc.vector.scalar_tensor_tensor(q2[:, :, :], a2[:, :, :], 1.0, et[:, :, :], ALU.add, ALU.mult).then_inc(sq, 1)
            c.link(tt(h[:, :, :], ea[:, :, :], m.prm[:, :, R_H0:R_H0 + 8], ALU.mult))
            v.wait_ge(sq, 2)
            c.link(tt(m1[:, :, :], m1[:, :, :], q2[:, :, :], ALU.mult))
            c.link(tt(h[:, :, :], h[:, :, :], m1[:, :, :], ALU.add))
            c.link(nc.vector.tensor_copy(m.out_t[:, :, 4:12], h[:, :, :]))
            nc.vector.tensor_copy(m.out_t[:, :, 12:20], u).then_inc(cp, 1)
            c.link(nc.vector.scalar_tensor_tensor(gz[:, :, :], m.gth_s[:, NMH:NI, :], 1.0, m.gh_s[:, NMH:NI, :], ALU.add, ALU.mult))
            tt(m.zs[:, NMH:NI, :], gz[:, :, :], h[:, :, :], ALU.mult)
            v.wait_ge(tr, 1)
            nc.vector.tensor_copy(states[0:20, 0:512], m.bank[2][0:20, :])
            c.link(nc.vector.tensor_copy(states[0:20, 512:1024], m.bank[3][0:20, :]))
            v.sem_inc(ev, 1)


def sample_mem_phase(nc, m, sem, l, A):
    P = f"sm{l}_"
    ldk, ldv = [sem(P + f"ldk{i}") for i in range(2)], sem(P + "ldv")
    kt_d, kt_e, s_d, s_e, t_d, m_r, e_d, p_r, pt_d, pt_e, o_d, ch = (sem(P + s) for s in
        ("kt_d", "kt_e", "s_d", "s_e", "t_d", "m_r", "e_d", "p_r", "pt_d", "pt_e", "o_d", "ch"))
    N = NMH * NS
    H = m.LO
    kb = [m.at(P + f"k{i}", [128, 2, DMEM], H + 4096 * i) for i in range(2)]
    kt = [m.at(P + f"kt{i}", [128, NMH, M], H + 8192 + 4096 * i) for i in range(2)]
    vb = m.at(P + "v", [128, NS, 2, DMEM], H + 16384)
    sT = m.at(P + "sT", [128, 2, N], H + 49152)
    pT = m.at(P + "pT", [128, 2, N], H + 49152 + 256)
    pr = m.at(P + "p", [N, M], H + 49152 + 512)
    gz = m.at(P + "gz", [128, NMH, NS], H + 49152 + 1536)
    st = m.at(P + "st", [N, 8], H + 49152 + 1664)
    b0, b1, b2, b3, b4 = m.bank[0], m.bank[1], m.bank[2], m.bank[3], m.bank[4]
    with nc.Block() as block:
        @block.sync
        def _(s):
            for b in range(NS):
                if b >= 2:
                    s.wait_ge(kt_d, b - 1)
                s.dma_start(kb[b % 2][:, :, :], A["cache_mem_k"][l, b].rearrange("(t p) h d -> p t (h d)", p=128)).then_inc(ldk[b % 2], 16)
                s.dma_start(vb[:, b, :, :], A["cache_mem_v"][l, b].rearrange("(t p) h d -> p t (h d)", p=128)).then_inc(ldv, 16)

        @block.tensor
        def _(pe):
            def scores(b):
                pe.wait_ge(kt_e, 2 * (b + 1))
                for h in range(NMH):
                    for t in range(2):
                        last = nc.tensor.matmul(b4[:, t * N + h * NS + b:t * N + h * NS + b + 1], kt[b % 2][:, h, t * 128:(t + 1) * 128],
                                                m.bs[:, h, b:b + 1], start=True, stop=True)
                last.then_inc(s_d, 1)

            for b in range(NS):
                pe.wait_ge(ldk[b % 2], 16 * (b // 2 + 1))
                if b >= 2:
                    pe.wait_ge(kt_e, 2 * (b - 1))
                for h in range(NMH):
                    for t in range(2):
                        last = nc.tensor.transpose(m.bank[2 * (b % 2) + h // 2][:, (h % 2) * M + t * 128:(h % 2) * M + (t + 1) * 128],
                                                   kb[b % 2][:, t, h * 128:(h + 1) * 128], m.ident[:, :])
                last.then_inc(kt_d, 1)
                if b:
                    scores(b - 1)
            scores(NS - 1)
            pe.wait_ge(s_e, 1)
            for t in range(2):
                last = nc.tensor.transpose(b0[0:N, t * 128:(t + 1) * 128], sT[:, t, :], m.ident[:, :])
            last.then_inc(t_d, 1)
            pe.wait_ge(p_r, 1)
            for t in range(2):
                last = nc.tensor.transpose(b1[:, t * N:(t + 1) * N], pr[:, t * 128:(t + 1) * 128], m.ident[0:N, 0:N])
            last.then_inc(pt_d, 1)
            pe.wait_ge(pt_e, 1)
            pe.wait_ge(ldv, 16 * NS)
            for h in range(NMH):
                for b in range(NS):
                    j = h * NS + b
                    for t in range(2):
                        last = nc.tensor.matmul(b2[:, j:j + 1], vb[:, b, t, h * 128:(h + 1) * 128], pT[:, t, j:j + 1], start=(t == 0), stop=(t == 1))
            last.then_inc(o_d, 1)

        @block.scalar
        def _(act):
            for b in range(NS):
                act.wait_ge(kt_d, b + 1)
                if b >= 2:
                    act.wait_ge(s_d, b - 1)
                for h in range(2):
                    nc.scalar.activation(kt[b % 2][:, 2 * h:2 * h + 2, :], m.bank[2 * (b % 2) + h][:, :].rearrange("p (h k) -> p h k", h=2),
                                         ACT.Copy).then_inc(kt_e, 1)
            act.wait_ge(m_r, 1)
            nc.scalar.activation(pr[:, :], b0[0:N, 0:M], ACT.Exp, bias=st[:, 1:2], scale=MEM_SCALE, accum_out=st[:, 2:3]).then_inc(e_d, 1)

        @block.vector
        def _(v):
            c = Chain(v, ch)
            v.wait_ge(s_d, NS)
            nc.vector.tensor_copy(sT[:, :, :], b4[:, 0:2 * N].rearrange("p (t n) -> p t n", t=2)).then_inc(s_e, 1)
            v.wait_ge(t_d, 1)
            c.link(nc.vector.reduce_max(st[:, 0:1], b0[0:N, 0:M], AX_X))
            nc.vector.tensor_scalar(st[:, 1:2], st[:, 0:1], -MEM_SCALE, None, ALU.mult).then_inc(m_r, 1)
            v.wait_ge(e_d, 1)
            c.link(nc.vector.reciprocal(st[:, 3:4], st[:, 2:3]))
            nc.vector.tensor_scalar(pr[:, :], pr[:, :], st[:, 3:4], None, ALU.mult).then_inc(p_r, 1)
            v.wait_ge(pt_d, 1)
            nc.vector.tensor_copy(pT[:, :, :], b1[:, 0:2 * N].rearrange("p (t n) -> p t n", t=2)).then_inc(pt_e, 1)
            c.link(nc.vector.scalar_tensor_tensor(gz[:, :, :], m.gth_s[:, 0:NMH, :], 1.0, m.gh_s[:, 0:NMH, :], ALU.add, ALU.mult))
            v.wait_ge(o_d, 1)
            nc.vector.tensor_tensor(m.zs[:, 0:NMH, :], gz[:, :, :], b2[:, 0:N].rearrange("p (h s) -> p h s", h=NMH), ALU.mult)


def kv_phase(nc, m, sem, A, outs):
    ldw, tab, st = sem("kv_ldw"), sem("kv_tab"), sem("kv_st")
    whi, wlo, hhi, hlo, mmd, kr, kvv, tr, ev, ch, zz = (sem("kv_" + s) for s in ("whi", "wlo", "hhi", "hlo", "mmd", "kr", "kvv", "tr", "ev", "ch", "zz"))
    H = m.HI
    NK = 256
    raw = m.at("kv_raw", [128, KT, NK], H)
    wl = m.at("kv_wl", [128, KT, NK], H, F32R)
    wh = m.at("kv_wh", [128, KT, NK], H + 8192, F32R)
    hh = [m.at(f"kv_hh{i}", [128, KT, 128], H + 16384 + 4096 * i, F32R) for i in range(2)]
    hl = [m.at(f"kv_hl{i}", [128, KT, 128], H + 24576 + 4096 * i, F32R) for i in range(2)]
    cs = m.at("kv_cs", [128, 2, TT + 1, 32], H + 32768)
    t1 = m.at("kv_t1", [128, 2, 2, 32], H + 32768 + 8704)
    t2 = m.at("kv_t2", [128, 2, 2, 32], H + 32768 + 8704 + 512)
    kn = [m.at(f"kv_kn{i}", [128, 2, 2, 32], H + 32768 + 8704 + 1024 + 512 * i) for i in range(2)]
    vlast = m.kV
    g = lambda k: m.prm[:, k, R_KVG:R_KVG + 1]
    rows = lambda t: 128 if t < TT else NS
    kvb = [m.bank[0], m.bank[1]]
    with nc.Block() as block:
        @block.sync
        def _(s):
            s.dma_start(raw[:, :, :], A["w_kv"].rearrange("(k p) n -> p k n", p=128)).then_inc(ldw, 16)
            s.dma_start(cs[:, :, :, :], A["rope_k"]).then_inc(tab, 16)
            s.dma_start(outs["wk_s"][:, 0:W - 1], A["cache_win_k"][:, 1:W]).then_inc(st, 16)
            s.dma_start(outs["wv_s"][:, 0:W - 1], A["cache_win_v"][:, 1:W]).then_inc(st, 16)
            s.wait_ge(kr, TT)
            s.dma_start(outs["wk_p"][0].rearrange("w g d -> w (g d)"), kn[(TT - 1) % 2][:, :, :, :].rearrange("p g h d -> p (g h d)")).then_inc(st, 16)
            s.wait_ge(kvv, TT)
            s.dma_start(outs["wv_p"][0].rearrange("w g d -> w (g d)"), m.kV[:, TT, :]).then_inc(st, 16)
            s.wait_ge(kvv, TT + 2)
            s.dma_start(outs["wk_s"][:, W - 1].rearrange("b g d -> b (g d)"), m.knew[0:NS, 0:128]).then_inc(st, 16)
            s.dma_start(outs["wv_s"][:, W - 1].rearrange("b g d -> b (g d)"), m.knew[0:NS, 128:256]).then_inc(st, 16)
            s.wait_ge(st, 96)

        @block.gpsimd
        def _(gp):
            gp.memset(m.kT[:, 0:128], 0.0).then_inc(zz, 1)
            gp.memset(m.kV[:, 0, :], 0.0).then_inc(zz, 1)

        @block.scalar
        def _(act):
            act.wait_ge(ldw, 16)
            nc.scalar.activation(wh[:, :, :], raw[:, :, :], ACT.Copy).then_inc(whi, 1)
            for t in range(TT + 1):
                n = rows(t)
                if t >= 2:
                    act.wait_ge(mmd, t - 1)
                for k in range(KT):
                    nc.scalar.activation(hh[t % 2][:, k, 0:n], m.hn[:, k, t * 128:t * 128 + n], ACT.Copy, scale=g(k)).then_inc(hhi, 1)

        @block.vector
        def _(v):
            c = Chain(v, ch)
            v.wait_ge(whi, 1)
            nc.vector.tensor_tensor(wl[:, :, :], raw[:, :, :], wh[:, :, :].bitcast(F32), ALU.subtract).then_inc(wlo, 1)
            v.wait_ge(tab, 16)

            def rope(t):
                n, ps = rows(t), kvb[t % 2]
                v.wait_ge(mmd, t + 1)
                if t:
                    v.wait_ge(kr, t)
                k = ps[0:n, 0:128].rearrange("p (g h d) -> p g h d", g=2, h=2)
                cb, sb = (cs[0:n, j, t, :].unsqueeze(1).broadcast_to([n, 2, 32]) for j in range(2))
                for h in range(2):
                    nc.vector.tensor_tensor(t1[0:n, :, h, :], k[:, :, h, :], cb, ALU.mult)
                    r = nc.vector.tensor_tensor(t2[0:n, :, h, :], k[:, :, 1 - h, :], sb, ALU.mult)
                c.link(r)
                out = kn[t % 2][0:n] if t < TT else m.knew[0:n, 0:128].rearrange("p (g h d) -> p g h d", g=2, h=2)
                if t >= 2:
                    v.wait_ge(tr, t - 1)
                for h, op in ((0, ALU.subtract), (1, ALU.add)):
                    r = nc.vector.tensor_tensor(out[:, :, h, :], t1[0:n, :, h, :], t2[0:n, :, h, :], op)
                if t < TT:
                    r.then_inc(kr, 1)
                else:
                    r.then_inc(kvv, 1)
                nc.vector.tensor_copy(m.kV[:, t + 1, :] if t < TT else m.knew[0:n, 128:256], ps[0:n, 128:256]).then_inc(kvv, 1)

            def evac(t):
                v.wait_ge(tr, t + 1)
                nc.vector.tensor_copy(m.kT[:, (t + 1) * 128:(t + 2) * 128], m.bank[2 + t % 2][:, 0:128]).then_inc(ev, 1)

            for t in range(TT + 1):
                n = rows(t)
                if t >= 2:
                    v.wait_ge(mmd, t - 1)
                for k in range(KT):
                    v.wait_ge(hhi, KT * t + k + 1)
                    r = nc.vector.scalar_tensor_tensor(hl[t % 2][:, k, 0:n], m.hn[:, k, t * 128:t * 128 + n], g(k),
                                                       hh[t % 2][:, k, 0:n].bitcast(F32), ALU.mult, ALU.subtract)
                r.then_inc(hlo, 1)
                if t >= 1:
                    rope(t - 1)
                if t >= 2:
                    evac(t - 2)
            rope(TT)
            evac(TT - 1)

        @block.tensor
        def _(pe):
            pe.wait_ge(wlo, 1)

            def kt_tile(t):
                pe.wait_ge(kr, t + 1)
                if t >= 2:
                    pe.wait_ge(ev, t - 1)
                nc.tensor.transpose(m.bank[2 + t % 2][:, 0:128], kn[t % 2][:, :, :, :].rearrange("p g h d -> p (g h d)"), m.ident[:, :]).then_inc(tr, 1)

            for t in range(TT + 1):
                n = rows(t)
                pe.wait_ge(hlo, t + 1)
                if t >= 2:
                    pe.wait_ge(kvv, t - 1)
                for k in range(KT):
                    a, b = hh[t % 2][:, k, 0:n], hl[t % 2][:, k, 0:n]
                    for q, (s_, r_) in enumerate(((a, wh), (a, wl), (b, wh))):
                        last = nc.tensor.matmul(kvb[t % 2][0:n, 0:NK], s_, r_[:, k, :], start=(k == 0 and q == 0), stop=(k == KT - 1 and q == 2))
                last.then_inc(mmd, 1)
                if t >= 1:
                    kt_tile(t - 1)


def sample_window_phase(nc, m, sem, A):
    ld, sw, kt_d, kt_e, q_r, s_d, s_e, t_d, m_r, e_d, p_r, pt_d, pt_e, o_d, ch, k0 = (sem("sw_" + s) for s in
        "ld sw kt_d kt_e q_r s_d s_e t_d m_r e_d p_r pt_d pt_e o_d ch k0".split())
    H = m.HI
    kw = m.at("sw_k", [128, NS, 128], H)
    vw = m.at("sw_v", [128, NS, 128], H + 4096)
    kt = m.at("sw_kt", [128, NS, 128], H + 8192)
    qr = m.at("sw_qr", [128, KT, NS], H + 12288)
    q1 = m.at("sw_q1", [128, KT, NS], H + 12544)
    qs = m.at("sw_qs", [128, KT, NS], H + 12800)
    cs = m.at("sw_cs", [128, 2], H + 13056)
    sT = m.at("sw_sT", [128, NS, 2, KT], H + 13312)
    pr = m.at("sw_p", [128, 128], H + 13824)
    pT = m.at("sw_pT", [128, 128], H + 14336)
    gz = m.at("sw_gz", [128, KT, NS], H + 14848)
    st = m.at("sw_st", [128, 8], H + 15104)
    u = m.bs[:, NMH:NI, :]
    with nc.Block() as block:
        @block.sync
        def _(s):
            for j, (dst, src) in enumerate(((kw, "cache_win_k"), (vw, "cache_win_v"))):
                s.dma_start(dst[1:128, :, :], A[src][:, 1:W].rearrange("b w g d -> w b (g d)")).then_inc(ld, 16)
                for b in range(NS):
                    s.dma_start(dst[0:1, b, :], m.knew[b:b + 1, j * 128:(j + 1) * 128]).then_inc(ld, 16)
            s.dma_start(cs[:, :], A["rope_q"][:, :, T], allow_slow_non_contiguous=True).then_inc(sw, 16)
            for r in range(4):
                s.dma_start(qr[32 * r:32 * r + 32, :, :], u[32 * (r ^ 1):32 * (r ^ 1) + 32, :, :]).then_inc(sw, 16)

        @block.tensor
        def _(pe):
            pe.wait_ge(ld, 16 * 2 * (NS + 1))
            for b in range(NS):
                last = nc.tensor.transpose(m.bank[b // 4][:, (b % 4) * 128:(b % 4 + 1) * 128], kw[:, b, :], m.ident[:, :])
            last.then_inc(kt_d, 1)
            pe.wait_ge(kt_e, 2)
            pe.wait_ge(q_r, 1)
            for g in range(2):
                for b in range(NS):
                    last = nc.tensor.matmul(m.bank[2 + g][:, b * 8:b * 8 + 8], kt[64 * g:64 * g + 64, b, :], qs[64 * g:64 * g + 64, :, b], start=True, stop=True)
            last.then_inc(s_d, 1)
            pe.wait_ge(s_e, 1)
            nc.tensor.transpose(m.bank[0][:, 0:128], sT[:, :, :, :].rearrange("p b g j -> p (b g j)"), m.ident[:, :]).then_inc(t_d, 1)
            pe.wait_ge(p_r, 1)
            nc.tensor.transpose(m.bank[1][:, 0:128], pr[:, :], m.ident[:, :]).then_inc(pt_d, 1)
            pe.wait_ge(pt_e, 1)
            for g in range(2):
                for b in range(NS):
                    last = nc.tensor.matmul(m.bank[4][64 * g:64 * g + 64, b * 8:b * 8 + 8], vw[:, b, 64 * g:64 * g + 64],
                                            pT[:, b * 16 + g * 8:b * 16 + g * 8 + 8], start=True, stop=True)
            last.then_inc(o_d, 1)

        @block.scalar
        def _(act):
            act.wait_ge(kt_d, 1)
            for h in range(2):
                nc.scalar.activation(kt[:, 4 * h:4 * h + 4, :], m.bank[h][:, :].rearrange("p (b k) -> p b k", b=4), ACT.Copy).then_inc(kt_e, 1)
            act.wait_ge(m_r, 2)
            nc.scalar.activation(st[:, 4:5], m.sink_col[:, :], ACT.Exp, bias=st[:, 2:3])
            nc.scalar.activation(pr[:, :], m.bank[0][:, 0:128], ACT.Exp, bias=st[:, 2:3], accum_out=st[:, 3:4]).then_inc(e_d, 1)

        @block.vector
        def _(v):
            c = Chain(v, ch)
            v.wait_ge(sw, 80)
            c.link(nc.vector.tensor_scalar(q1[:, :, :], qr[:, :, :], cs[:, 1:2], None, ALU.mult))
            nc.vector.scalar_tensor_tensor(qs[:, :, :], u, cs[:, 0:1], q1[:, :, :], ALU.mult, ALU.add).then_inc(q_r, 1)
            v.wait_ge(s_d, 1)
            nc.vector.tensor_copy(sT[:, :, 0, :], m.bank[2][:, 0:64].rearrange("p (b j) -> p b j", b=NS))
            nc.vector.tensor_copy(sT[:, :, 1, :], m.bank[3][:, 0:64].rearrange("p (b j) -> p b j", b=NS)).then_inc(s_e, 1)
            v.wait_ge(t_d, 1)
            c.link(nc.vector.reduce_max(st[:, 0:1], m.bank[0][:, 0:128], AX_X))
            c.link(nc.vector.tensor_tensor(st[:, 1:2], st[:, 0:1], m.sink_col[:, :], ALU.max))
            nc.vector.tensor_scalar(st[:, 2:3], st[:, 1:2], -1.0, None, ALU.mult).then_inc(m_r, 2)
            v.wait_ge(e_d, 1)
            c.link(nc.vector.tensor_tensor(st[:, 5:6], st[:, 3:4], st[:, 4:5], ALU.add))
            c.link(nc.vector.reciprocal(st[:, 6:7], st[:, 5:6]))
            nc.vector.tensor_scalar(pr[:, :], pr[:, :], st[:, 6:7], None, ALU.mult).then_inc(p_r, 1)
            v.wait_ge(pt_d, 1)
            nc.vector.tensor_copy(pT[:, :], m.bank[1][:, 0:128]).then_inc(pt_e, 1)
            c.link(nc.vector.scalar_tensor_tensor(gz[:, :, :], m.gth_s[:, NMH:NI, :], 1.0, m.gh_s[:, NMH:NI, :], ALU.add, ALU.mult))
            v.wait_ge(o_d, 1)
            nc.vector.tensor_tensor(m.zs[:, NMH:NI, :], gz[:, :, :], m.bank[4][:, 0:64].rearrange("p (b j) -> p j b", b=NS), ALU.mult)


def output_phase(nc, m, sem, l, A, outs):
    P = f"op{l}_"
    V0 = m.V0
    stage = [m.at(P + f"st{i}", [128, D], V0 + 4096 * i) for i in range(4)]
    zr = [m.at(P + f"zr{i}", [128, NI, 128], V0 + 6144 * i) for i in range(2)]
    zl = [m.at(P + f"zl{i}", [128, NI, 128], V0 + 6144 * i, F32R) for i in range(2)]
    zh = [m.at(P + f"zh{i}", [128, NI, 128], V0 + 12288 + 6144 * i, F32R) for i in range(2)]
    x = [m.at(P + f"x{i}", [128, D], V0 + 24576 + 4096 * i) for i in range(3)]
    y = [m.at(P + f"y{i}", [128, D], V0 + 36864 + 4096 * i) for i in range(2)]
    fg = m.at(P + "fg", [128, D], V0 + 45056)
    st = m.stat
    ldw = [sem(P + f"ldw{i}") for i in range(4)]
    ldz = [sem(P + f"ldz{i}") for i in range(2)]
    ldx = [sem(P + f"ldx{i}") for i in range(3)]
    sx = [sem(P + f"sx{i}") for i in range(3)]
    whi, wlo, zhi, zlo, mmd, xn, ss, yn, tr, hev, ch, fgl, zsp = (sem(P + s) for s in
        "whi wlo zhi zlo mmd xn ss yn tr hev ch fgl zsp".split())
    rows = lambda t: 128 if t < TT else NS

    def wrows(k):
        if k < NMH:
            return [(D + 128 * k, 128, 0)]
        j = k - NMH
        return [(128 * j, 128, 0)] if l == 0 else [(64 * j, 64, 0), (512 + 64 * j, 64, 64)]

    with nc.Block() as block:
        @block.sync
        def _(s):
            for k in range(NI):
                if k >= 4:
                    s.wait_ge(wlo, k - 3)
                for r0, n, o in wrows(k):
                    s.dma_start(stage[k % 4][o:o + n, :], A["w_out"][l, r0:r0 + n, :]).then_inc(ldw[k % 4], 16)
        
        @block.scalar
        def _(act):
            seen = [0] * 4
            for k in range(NI):
                seen[k % 4] += 16 * len(wrows(k))
                act.wait_ge(ldw[k % 4], seen[k % 4])
                nc.scalar.activation(m.wo_hi[:, k, :], stage[k % 4][:, :], ACT.Copy).then_inc(whi, 1)

        @block.vector
        def _(v):
            for k in range(NI):
                v.wait_ge(whi, k + 1)
                nc.vector.tensor_tensor(m.wo_lo[:, k, :], stage[k % 4][:, :], m.wo_hi[:, k, :].bitcast(F32), ALU.subtract).then_inc(wlo, 1)
            c = Chain(v, zsp)
            nc.vector.tensor_copy(m.zs_hi[:, :, :], m.zs[:, :, :]).then_inc(zsp, 1)
            v.wait_ge(zsp, 1)
            nc.vector.tensor_tensor(m.zs_lo[:, :, :], m.zs[:, :, :], m.zs_hi[:, :, :].bitcast(F32), ALU.subtract)

    xsrc = lambda t: ((A["x_prompt"][0, t * 128:(t + 1) * 128, :] if t < TT else A["x_sample"].rearrange("b s d -> (b s) d")) if l == 0
                      else m.x1_d[t * 128:t * 128 + rows(t), :])
    xdst = lambda t: (m.x1_d[t * 128:t * 128 + rows(t), :] if l == 0
                      else (outs["y_p"][0, t * 128:(t + 1) * 128, :] if t < TT else outs["y_s"].rearrange("b s d -> (b s) d")))
    with nc.Block() as block:
        @block.sync
        def _(s):
            if l == 1:
                s.dma_start(fg[:, :], A["final_g"].unsqueeze(0).broadcast_to([128, D])).then_inc(fgl, 16)

            def load(t):
                if t < TT:
                    if t >= 2:
                        s.wait_ge(mmd, 2 * (t - 1))
                    s.dma_start(zr[t % 2][:, :, :], m.z_d[:, :, t * 128:(t + 1) * 128].rearrange("k p t -> p k t")).then_inc(ldz[t % 2], 16)
                if t >= 3:
                    s.wait_ge(yn, t - 2)
                    if l == 0:
                        s.wait_ge(sx[t % 3], 16 * (t // 3))
                s.dma_start(x[t % 3][0:rows(t), :], xsrc(t)).then_inc(ldx[t % 3], 16)

            load(0)
            load(1)
            for t in range(TT + 1):
                if l == 0:
                    s.wait_ge(xn, 2 * (t + 1))
                    s.dma_start(xdst(t), x[t % 3][0:rows(t), :]).then_inc(sx[t % 3], 16)
                if t + 2 <= TT:
                    load(t + 2)
                if l == 1:
                    s.wait_ge(yn, t + 1)
                    s.dma_start(xdst(t), y[t % 2][0:rows(t), :]).then_inc(sx[t % 2], 16)
            for i in range(3):
                n = len([t for t in range(TT + 1) if t % (3 if l == 0 else 2) == i]) if (l == 0 or i < 2) else 0
                if n:
                    s.wait_ge(sx[i], 16 * n)

        @block.scalar
        def _(act):
            def split(t):
                act.wait_ge(ldz[t % 2], 16 * (t // 2 + 1))
                if t >= 2:
                    act.wait_ge(mmd, 2 * (t - 1))
                nc.scalar.activation(zh[t % 2][:, :, :], zr[t % 2][:, :, :], ACT.Copy).then_inc(zhi, 1)

            split(0)
            for t in range(TT + 2):
                if t + 1 < TT:
                    split(t + 1)
                if l == 0 and t >= 1:
                    u = t - 1
                    act.wait_ge(tr, u + 1)
                    for h in range(2):
                        i = nc.scalar.activation(m.hn[:, 4 * h:4 * h + 4, u * 128:u * 128 + rows(u)],
                                                 m.bank[4 + 2 * (u % 2) + h][:, :].rearrange("p (k c) -> p k c", k=4)[:, :, 0:rows(u)], ACT.Copy)
                    i.then_inc(hev, 1)
                if t <= TT:
                    n, p = rows(t), t % 2
                    act.wait_ge(xn, 2 * (t + 1))
                    if t >= 2:
                        if l == 0:
                            act.wait_ge(tr, t - 1)
                        else:
                            act.wait_ge(sx[p], 16 * (t // 2))
                    nc.scalar.activation(y[p][0:n, :], x[t % 3][0:n, :], ACT.Square, accum_out=st[0:n, p:p + 1]).then_inc(ss, 1)
                    act.wait_ge(ss, 2 * t + 1)
                    nc.scalar.activation(st[0:n, 2 + p:3 + p], st[0:n, p:p + 1], ACT.Sqrt, bias=m.eps[0:n, :], scale=1.0 / D).then_inc(ss, 1)

        @block.vector
        def _(v):
            c = Chain(v, ch)

            def split(t):
                v.wait_ge(zhi, t + 1)
                nc.vector.tensor_tensor(zl[t % 2][:, :, :], zr[t % 2][:, :, :], zh[t % 2][:, :, :].bitcast(F32), ALU.subtract).then_inc(zlo, 1)

            split(0)
            for t in range(TT + 1):
                n, p = rows(t), t % 2
                if t + 1 < TT:
                    split(t + 1)
                v.wait_ge(ldx[t % 3], 16 * (t // 3 + 1))
                for h in range(2):
                    v.wait_ge(mmd, 2 * t + h + 1)
                    xs = x[t % 3][0:n, h * 512:(h + 1) * 512]
                    nc.vector.tensor_tensor(xs, xs, m.bank[2 * p + h][0:n, :], ALU.add).then_inc(xn, 1)
                v.wait_ge(ss, 2 * t + 2)
                v.wait_ge(xn, 2 * t + 2)
                c.link(nc.vector.reciprocal(st[0:n, 4 + p:5 + p], st[0:n, 2 + p:3 + p]))
                if l == 0:
                    nc.vector.tensor_scalar(y[p][0:n, :], x[t % 3][0:n, :], st[0:n, 4 + p:5 + p], None, ALU.mult).then_inc(yn, 1)
                else:
                    if t == 0:
                        v.wait_ge(fgl, 16)
                    nc.vector.scalar_tensor_tensor(y[p][0:n, :], x[t % 3][0:n, :], st[0:n, 4 + p:5 + p], fg[0:n, :], ALU.mult, ALU.mult).then_inc(yn, 1)

        @block.tensor
        def _(pe):
            def flip(u):
                pe.wait_ge(yn, u + 1)
                if u >= 2:
                    pe.wait_ge(hev, u - 1)
                n = rows(u)
                for k in range(KT):
                    last = nc.tensor.transpose(m.bank[4 + 2 * (u % 2) + k // 4][:, (k % 4) * 128:(k % 4) * 128 + n],
                                               y[u % 2][0:n, k * 128:(k + 1) * 128], m.ident[0:n, 0:n])
                last.then_inc(tr, 1)

            for t in range(TT + 1):
                n, p = rows(t), t % 2
                if t < TT:
                    pe.wait_ge(zlo, t + 1)
                if t >= 2:
                    pe.wait_ge(xn, 2 * (t - 1))
                for h in range(2):
                    for k in range(NI):
                        a, b = (zh[p][:, k, :], zl[p][:, k, :]) if t < TT else (m.zs_hi[:, k, :], m.zs_lo[:, k, :])
                        wh, wl = m.wo_hi[:, k, h * 512:(h + 1) * 512], m.wo_lo[:, k, h * 512:(h + 1) * 512]
                        for q, (s_, r_) in enumerate(((a, wh), (a, wl), (b, wh))):
                            last = nc.tensor.matmul(m.bank[2 * p + h][0:n, :], s_, r_, start=(k == 0 and q == 0), stop=(k == NI - 1 and q == 2))
                    last.then_inc(mmd, 1)
                    if l == 0 and h == 0 and t >= 1:
                        flip(t - 1)
            if l == 0:
                flip(TT)


def build(nc, A, outs):
    with ExitStack() as ctx:
        m = Mem(nc, ctx)
        held = []

        def sem(name):
            held.append(nc.alloc_semaphore(name=name))
            return held[-1]

        def recycle():
            nc.clear_and_free_semaphores(held)
            held.clear()
            nc.all_engine_barrier()

        A["mem_v"] = outs["mem_v"]
        setup_phase(nc, m, sem, A)
        memory_phase(nc, m, sem, A, outs)
        input_norm_phase(nc, m, sem, A)
        split_phase(nc, m, sem, 0)
        recycle()
        item_phase(nc, m, sem, 0, A)
        sample_mem_phase(nc, m, sem, 0, A)
        sample_lru_phase(nc, m, sem, A, outs)
        output_phase(nc, m, sem, 0, A, outs)
        recycle()
        kv_phase(nc, m, sem, A, outs)
        split_phase(nc, m, sem, 1)
        item_phase(nc, m, sem, 1, A)
        sample_mem_phase(nc, m, sem, 1, A)
        recycle()
        sample_window_phase(nc, m, sem, A)
        output_phase(nc, m, sem, 1, A, outs)


_INS = ["x_prompt", "x_sample", "cache_mem_k", "cache_mem_v", "state_lru_h", "state_conv", "cache_win_k", "cache_win_v",
        "mem_prompt", "norm_g", "w_in", "w_out", "mem_norm_g", "w_mem_kv", "conv_w", "conv_b", "lru_wa", "lru_ba",
        "lru_wx", "lru_bx", "lru_lambda", "kv_norm_g", "w_kv", "sinks", "final_g"]
_OUTS = [("y_p", (1, T, D)), ("y_s", (NS, 1, D)), ("mem_k", (2, 1, M, NMH, 128)), ("mem_v", (2, 1, M, NMH, 128)),
         ("lru_p", (1, 1, D)), ("conv_p", (1, 1, 3, D)), ("wk_p", (1, W, 2, HD)), ("wv_p", (1, W, 2, HD)),
         ("lru_s", (1, NS, D)), ("conv_s", (1, NS, 3, D)), ("wk_s", (NS, W, 2, HD)), ("wv_s", (NS, W, 2, HD))]


def rope_tables():
    half = HD // 2
    inv = (np.float32(10000.0) ** (-np.arange(half, dtype=np.float32) / np.float32(half))).astype(np.float32)
    pos = np.concatenate([np.arange(T), np.full(128, T)]).astype(np.float32)
    ang = pos[:, None] * inv[None, :]
    cos, sin = np.cos(ang), np.sin(ang)
    q = np.empty((128, 2, TA), np.float32)
    for r in range(4):
        q[32 * r:32 * r + 32, 0] = cos[:TA].T
        q[32 * r:32 * r + 32, 1] = sin[:TA].T * (-1.0 if r % 2 == 0 else 1.0)
    q *= np.float32(HD ** -0.5)
    k = np.stack([cos, sin]).reshape(2, TT + 1, 128, half).transpose(2, 0, 1, 3)
    return q, np.ascontiguousarray(k, np.float32)


def kernel(**inputs):
    import concourse.bacc as _bacc
    from concourse.bass_utils import run_bass_kernel_spmd as _run

    nc = _bacc.Bacc("TRN2", target_bir_lowering=False, num_devices=1, dynamic_dma_scratch_size=4096)
    arrays, A = {}, {}
    rq, rk = rope_tables()
    for name, a in [(n, np.ascontiguousarray(inputs[n])) for n in _INS] + [("rope_q", rq), ("rope_k", rk)]:
        arrays[f"in_{name}"] = a
        A[name] = nc.dram_tensor(f"in_{name}", a.shape, mybir.dt.from_np(a.dtype), kind="ExternalInput").ap()
    outs = {n: nc.dram_tensor(f"out_{n}", s, F32, kind="ExternalOutput").ap() for n, s in _OUTS}
    build(nc, A, outs)
    r = _run(nc, [arrays], core_ids=[0])
    return tuple(r.results[0][f"out_{n}"] for n, _ in _OUTS)
```

```python
import numpy as np
import concourse.bass as bass
from concourse import mybir
from contextlib import ExitStack

F32 = mybir.dt.float32
F32R = mybir.dt.float32r
ALU = mybir.AluOpType
ACT = mybir.ActivationFunctionType
AX_X = mybir.AxisListType.X

D = 1024
KT = D // 128
T = 2048
TT = T // 128
NS = 8
TA = T + NS
CH = 512
NCH = T // CH
DIN = 3072
DMEM = 512
CAT = 1536
NI = CAT // 128
NMH = 4
M = 256
HD = 64
W = 128
NH = 16
EPS = 1e-6
NEG = -1e30
MEM_SCALE = 128 ** -0.5

R_CW, R_CB, R_BA, R_BX, R_LAM, R_G, R_KVG, R_MG, R_ST, R_H0, NR = 0, 4, 5, 6, 7, 8, 10, 11, 13, 37, 45


def ds(start, size):
    return slice(start, start + size) if isinstance(start, int) else bass.ds(start, size)


class Chain:

    def __init__(self, eng, sem, base=0):
        self.eng, self.sem, self.base, self.n = eng, sem, base, 0

    def link(self, ins):
        ins.then_inc(self.sem, 1)
        self.n += 1
        self.eng.wait_ge(self.sem, self.base + self.n)


class Mem:

    def __init__(self, nc, ctx):
        self.nc = nc
        base = 1152 + 32
        ctx.enter_context(nc.sbuf_tensor("fence", [128, (229344 - base) // 4], F32))
        self.HI = base
        self.WS = self.HI + KT * TA * 4
        self.LO = self.WS + 8 * KT * 128 * 4
        self.WK = self.LO + KT * TA * 4
        self.V0 = self.WK + 10048
        self.end = 229344

        def fixed(name, shape, dt=F32):
            place[0] += self.size(shape)
            return self.at(name, shape, place[0] - self.size(shape), dt)

        place = [self.WK]
        self.ident = fixed("ident", [128, 128])
        self.prm = fixed("prm", [128, KT, NR])
        self.dvp = fixed("dvp", [128, KT, 4])
        self.mask = fixed("mask", [128, 3, 128])
        self.sink_bc = fixed("sink_bc", [128, NH])
        self.sink_col = fixed("sink_col", [128, 1])
        self.eps = fixed("eps", [128, 1])
        self.stat = fixed("stat", [128, 64])
        self.bs = fixed("bs", [128, NI, NS])
        self.gth_s = fixed("gth_s", [128, NI, NS])
        self.gh_s = fixed("gh_s", [128, NI, NS])
        self.zs = fixed("zs", [128, NI, NS])
        self.out_t = fixed("out_t", [128, KT, 20])
        self.knew = fixed("knew", [128, 256])
        self.lru_par = fixed("lru_par", [128, 4])
        self.srow_st = [fixed(f"srow_st{p}", [128, 256]) for p in range(2)]
        self.zs_hi = fixed("zs_hi", [128, NI, NS], F32R)
        self.zs_lo = fixed("zs_lo", [128, NI, NS], F32R)
        assert place[0] <= self.V0, place[0] - self.V0
        self.hn = self.at("hn", [128, KT, TA], self.LO)
        self.hn_hi = self.at("hn_hi", [128, KT, TA], self.HI, F32R)
        self.hn_lo = self.at("hn_lo", [128, KT, TA], self.LO, F32R)
        s = KT * 128 * 4
        self.w_raw = [self.at(f"w_raw{p}", [128, KT, 2, 128], self.WS + p * 4 * s) for p in range(2)]
        self.w_lo = [self.at(f"w_lo{p}", [128, KT, 2, 128], self.WS + p * 4 * s, F32R) for p in range(2)]
        self.w_hi = [self.at(f"w_hi{p}", [128, KT, 2, 128], self.WS + (p * 4 + 2) * s, F32R) for p in range(2)]
        self.wo_hi = self.at("wo_hi", [128, NI, D], self.HI, F32R)
        self.wo_lo = self.at("wo_lo", [128, NI, D], self.HI + NI * D * 4, F32R)
        assert self.HI + 2 * NI * D * 4 <= self.LO
        self.kT = self.at("kT", [128, (TT + 1) * 128], self.V0 + 8192)
        self.kV = self.at("kV", [128, TT + 1, 128], self.V0 + 8192 + (TT + 1) * 512)
        self.kv_end = self.V0 + 8192 + 2 * (TT + 1) * 512
        self.bank = [ctx.enter_context(nc.psum_tensor(f"bank{i}", [128, 512], F32)) for i in range(8)]
        self.z_d = nc.dram_tensor("z_scratch", (NI, 128, T), F32).ap()
        self.x1_d = nc.dram_tensor("x1_scratch", (TA, D), F32).ap()
        self.srow_d = nc.dram_tensor("srow_scratch", (NS, 2 * CAT), F32).ap()
        self.kmt_d = nc.dram_tensor("kmt_scratch", (2, 128, NMH * M), F32).ap()

    @staticmethod
    def size(shape):
        return -(-int(np.prod(shape[1:])) * 4 // 32) * 32

    def at(self, name, shape, off, dt=F32):
        size = int(np.prod(shape[1:])) * 4
        assert off + size <= 229344, (name, off + size)
        return self.nc.alloc_sbuf_tensor_at(name, shape, dt, offset=off)


def bc(ap, n):
    return ap.unsqueeze(ap.ndim).broadcast_to(list(ap.shape) + [n])


def setup_phase(nc, m, sem, A):
    ld, ids, tr, ev = sem("su_ld"), sem("su_id"), sem("su_tr"), sem("su_ev")
    ch, ea, va = sem("su_ch"), sem("su_ea"), sem("su_va")
    rows = m.at("rows", [NR, D], m.V0)
    sp = m.at("sp", [128, 6, KT], m.V0 + 4096)
    ps = m.bank[0][:, :].rearrange("p (k r) -> p k r", k=KT)
    srcs = [(R_CW, 4, A["conv_w"][0]), (R_CB, 1, A["conv_b"]), (R_BA, 1, A["lru_ba"]), (R_BX, 1, A["lru_bx"]),
            (R_LAM, 1, A["lru_lambda"]), (R_G, 2, A["norm_g"]), (R_KVG, 1, A["kv_norm_g"].unsqueeze(0)),
            (R_MG, 2, A["mem_norm_g"]), (R_ST, 24, A["state_conv"][0].rearrange("b k d -> (b k) d")),
            (R_H0, 8, A["state_lru_h"][0])]
    nld = 16 * (len(srcs) + 1 + NS)
    with nc.Block() as block:
        @block.sync
        def _(sp_):
            for r, n, src in srcs:
                sp_.dma_start(rows[r:r + n, :], src).then_inc(ld, 16)
            sp_.dma_start(m.sink_bc[:, :], A["sinks"].broadcast_to([128, NH])).then_inc(ld, 16)
            for b in range(NS):
                sp_.dma_start(m.sink_col[b * NH:(b + 1) * NH, :], A["sinks"].rearrange("a h -> h a")).then_inc(ld, 16)
            sp_.wait_ge(ld, nld)

        @block.gpsimd
        def _(g):
            g.memset(m.ident[:, :], 0.0).then_inc(ids, 1)
            g.memset(m.mask[:, :, :], 0.0).then_inc(ids, 1)
            g.memset(m.eps[:, :], EPS).then_inc(ids, 1)
            g.wait_ge(ids, 3)
            g.affine_select(out=m.ident[:, :], in_=m.ident[:, :], compare_op=ALU.not_equal, fill=1.0,
                            base=0, pattern=[[-1, 128]], channel_multiplier=1).then_inc(ids, 1)
            g.memset(m.mask[:, 0, :], NEG).then_inc(ids, 1)
            g.affine_select(out=m.mask[:, 1, :], in_=m.mask[:, 1, :], compare_op=ALU.is_gt, fill=NEG,
                            base=0, pattern=[[1, 128]], channel_multiplier=-1).then_inc(ids, 1)
            g.affine_select(out=m.mask[:, 2, :], in_=m.mask[:, 2, :], compare_op=ALU.is_ge, fill=NEG,
                            base=0, pattern=[[-1, 128]], channel_multiplier=1).then_inc(ids, 1)
            g.wait_ge(ids, 7)

        @block.tensor
        def _(pe):
            pe.wait_ge(ld, nld)
            pe.wait_ge(ids, 4)
            for k in range(KT):
                last = nc.tensor.transpose(ps[:, k, 0:NR], rows[:, k * 128:(k + 1) * 128], m.ident[0:NR, 0:NR])
            last.then_inc(tr, 1)

        @block.scalar
        def _(act):
            act.wait_ge(ea, 2)
            nc.scalar.activation(sp[:, 1, :], sp[:, 0, :], ACT.Exp).then_inc(va, 1)

        @block.vector
        def _(v):
            c = Chain(v, ch)
            v.wait_ge(tr, 1)
            c.link(nc.vector.tensor_copy(m.prm[:, :, :], ps[:, :, 0:NR]))
            lam = m.prm[:, :, R_LAM]
            nc.vector.tensor_scalar(sp[:, 2, :], lam, -1.0, None, ALU.mult).then_inc(ea, 1)
            v.wait_ge(ea, 1)
            nc.vector.tensor_tensor(sp[:, 0, :], lam, sp[:, 2, :], ALU.min).then_inc(ea, 1)
            v.wait_ge(va, 1)
            c.link(nc.vector.tensor_scalar(sp[:, 3, :], sp[:, 1, :], 2.0, None, ALU.add))
            c.link(nc.vector.reciprocal(sp[:, 3, :], sp[:, 3, :]))
            c.link(nc.vector.tensor_tensor(sp[:, 3, :], sp[:, 3, :], sp[:, 1, :], ALU.mult))
            c.link(nc.vector.tensor_tensor(sp[:, 4, :], sp[:, 3, :], sp[:, 3, :], ALU.mult))
            c.link(nc.vector.tensor_scalar(sp[:, 5, :], sp[:, 4, :], 1.0 / 15, 1.0 / 13, ALU.mult, ALU.add))
            for q in (11, 9, 7, 5, 3, 1):
                c.link(nc.vector.tensor_tensor(sp[:, 5, :], sp[:, 5, :], sp[:, 4, :], ALU.mult))
                c.link(nc.vector.tensor_scalar(sp[:, 5, :], sp[:, 5, :], 1.0 / q, None, ALU.add))
            c.link(nc.vector.tensor_tensor(sp[:, 5, :], sp[:, 5, :], sp[:, 3, :], ALU.mult))
            c.link(nc.vector.tensor_scalar(sp[:, 2, :], sp[:, 2, :], 0.0, None, ALU.max))
            c.link(nc.vector.scalar_tensor_tensor(sp[:, 5, :], sp[:, 5, :], 2.0, sp[:, 2, :], ALU.mult, ALU.add))
            nc.vector.tensor_scalar(m.dvp[:, :, 0], sp[:, 5, :], -4.0, None, ALU.mult)
            nc.vector.tensor_scalar(m.dvp[:, :, 1], sp[:, 5, :], 4.0, None, ALU.mult)
            nc.vector.tensor_scalar(m.dvp[:, :, 2], m.prm[:, :, R_BA], 0.5, None, ALU.mult)
            nc.vector.tensor_scalar(m.dvp[:, :, 3], m.prm[:, :, R_BX], 0.5, None, ALU.mult)


def memory_phase(nc, m, sem, A, outs):
    ldx, ldw = sem("mm_ldx"), [sem(f"mm_ldw{i}") for i in range(4)]
    ss, x2, tr, hev, whi, wlo, hhi, hlo = (sem("mm_" + s) for s in ("ss", "x2", "tr", "hev", "whi", "wlo", "hhi", "hlo"))
    mmd, kvr, ktr, kte, st = (sem("mm_" + s) for s in ("mmd", "kvr", "ktr", "kte", "st"))
    ch = sem("mm_ch")
    V0 = m.V0
    x = m.at("mm_x", [128, 2, D], m.WS)
    junk = m.at("mm_junk", [128, D], m.WS + 8192)
    hnm = m.at("mm_hn", [128, KT, M], m.WS + 12288)
    hh = m.at("mm_hh", [128, KT, M], m.WS + 20480, F32R)
    hl = m.at("mm_hl", [128, KT, M], V0, F32R)
    stage = [m.at(f"mm_st{i}", [128, D], V0 + 8192 + 4096 * i) for i in range(4)]
    kv = [m.at(f"mm_kv{i}", [128, 2, D], V0 + 24576 + 8192 * i) for i in range(2)]
    ktb = [m.at(f"mm_kt{i}", [128, NMH, M], V0 + 40960 + 4096 * i) for i in range(2)]
    wh = m.at("mm_wh", [128, 2, KT, D], m.HI, F32R)
    wl = m.at("mm_wl", [128, 2, KT, D], m.LO, F32R)
    with nc.Block() as block:
        @block.sync
        def _(s):
            s.dma_start(x[:, :, :], A["mem_prompt"][0].rearrange("(t p) d -> p t d", p=128)).then_inc(ldx, 16)
            for q in range(2 * KT):
                l, k = q // KT, q % KT
                if q >= 4:
                    s.wait_ge(wlo, q - 3)
                s.dma_start(stage[q % 4][:, :], A["w_mem_kv"][l, k * 128:(k + 1) * 128, :]).then_inc(ldw[q % 4], 16)
            for l in range(2):
                for mt in range(2):
                    s.wait_ge(kvr, 2 * (2 * l + mt + 1))
                    for h, o in ((0, outs["mem_k"]), (1, outs["mem_v"])):
                        s.dma_start(o[l, 0].rearrange("m h d -> m (h d)")[mt * 128:(mt + 1) * 128, :],
                                    kv[l][:, mt, h * DMEM:(h + 1) * DMEM]).then_inc(st, 16)
            for l in range(2):
                s.wait_ge(kte, 2 * l + 2)
                s.dma_start(m.kmt_d[l], ktb[l][:, :, :].rearrange("p h m -> p (h m)")).then_inc(st, 16)
            s.wait_ge(st, 16 * 10)

        @block.scalar
        def _(act):
            act.wait_ge(ldx, 16)
            for t in range(2):
                nc.scalar.activation(junk[:, :], x[:, t, :], ACT.Square, accum_out=m.stat[:, t:t + 1]).then_inc(ss, 1)
                act.wait_ge(ss, t + 1)
            nc.scalar.activation(m.stat[:, 2:4], m.stat[:, 0:2], ACT.Sqrt, bias=m.eps[:, :], scale=1.0 / D).then_inc(ss, 1)
            for h in range(2):
                act.wait_ge(tr, h + 1)
                for t in range(2):
                    i = nc.scalar.activation(hnm[:, 4 * h:4 * h + 4, t * 128:(t + 1) * 128],
                                             m.bank[2 * h + t][:, :].rearrange("p (k c) -> p k c", k=4), ACT.Copy)
                i.then_inc(hev, 1)
            act.wait_ge(hev, 2)
            for q in range(2 * KT):
                l = q // KT
                if q % KT == 0:
                    for k in range(KT):
                        if q and k == 0:
                            act.wait_ge(mmd, 4)
                        nc.scalar.activation(hh[:, k, :], hnm[:, k, :], ACT.Copy, scale=m.prm[:, k, R_MG + l:R_MG + l + 1]).then_inc(hhi, 1)
                act.wait_ge(ldw[q % 4], 16 * (q // 4 + 1))
                nc.scalar.activation(wh[:, l, q % KT, :], stage[q % 4][:, :], ACT.Copy).then_inc(whi, 1)
            for i in range(4):
                act.wait_ge(ktr, i + 1)
                nc.scalar.activation(ktb[i // 2][:, 2 * (i % 2):2 * (i % 2) + 2, :],
                                     m.bank[6 + i % 2][:, :].rearrange("p (h c) -> p h c", h=2), ACT.Copy).then_inc(kte, 1)

        @block.vector
        def _(v):
            c = Chain(v, ch)
            v.wait_ge(ss, 3)
            c.link(nc.vector.reciprocal(m.stat[:, 4:6], m.stat[:, 2:4]))
            for t in range(2):
                nc.vector.tensor_scalar(x[:, t, :], x[:, t, :], m.stat[:, 4 + t:5 + t], None, ALU.mult).then_inc(x2, 1)

            def evac(i):
                l, mt, h = i // 4, i // 2 % 2, i % 2
                v.wait_ge(mmd, i + 1)
                nc.vector.tensor_copy(kv[l][:, mt, h * 512:(h + 1) * 512], m.bank[4 + i % 2][:, :]).then_inc(kvr, 1)

            v.wait_ge(hev, 2)
            for q in range(2 * KT):
                l, k = q // KT, q % KT
                if k == 0:
                    if l:
                        for i in range(4):
                            evac(i)
                    for k2 in range(KT):
                        v.wait_ge(hhi, l * KT + k2 + 1)
                        nc.vector.scalar_tensor_tensor(hl[:, k2, :], hnm[:, k2, :], m.prm[:, k2, R_MG + l:R_MG + l + 1],
                                                       hh[:, k2, :].bitcast(F32), ALU.mult, ALU.subtract).then_inc(hlo, 1)
                v.wait_ge(whi, q + 1)
                nc.vector.tensor_tensor(wl[:, l, k, :], stage[q % 4][:, :], wh[:, l, k, :].bitcast(F32), ALU.subtract).then_inc(wlo, 1)
            for i in range(4, 8):
                evac(i)

        @block.tensor
        def _(pe):
            for h in range(2):
                for t in range(2):
                    pe.wait_ge(x2, t + 1)
                    for k in range(4):
                        last = nc.tensor.transpose(m.bank[2 * h + t][:, k * 128:(k + 1) * 128],
                                                   x[:, t, (4 * h + k) * 128:(4 * h + k + 1) * 128], m.ident[:, :])
                last.then_inc(tr, 1)
            for i in range(8):
                l, mt, h = i // 4, i // 2 % 2, i % 2
                pe.wait_ge(hlo, KT * (l + 1))
                if i >= 2:
                    pe.wait_ge(kvr, i - 1)
                for k in range(KT):
                    pe.wait_ge(wlo, l * KT + k + 1)
                    a, b = hh[:, k, mt * 128:(mt + 1) * 128], hl[:, k, mt * 128:(mt + 1) * 128]
                    c, d = wh[:, l, k, h * 512:(h + 1) * 512], wl[:, l, k, h * 512:(h + 1) * 512]
                    for n, (p, q) in enumerate(((a, c), (a, d), (b, c))):
                        last = nc.tensor.matmul(m.bank[4 + i % 2][:, :], p, q, start=(k == 0 and n == 0), stop=(k == KT - 1 and n == 2))
                last.then_inc(mmd, 1)
            for i in range(4):
                l, hp = i // 2, i % 2
                pe.wait_ge(kvr, 4 * (l + 1))
                if i >= 2:
                    pe.wait_ge(kte, i - 1)
                for h in range(2):
                    for mt in range(2):
                        last = nc.tensor.transpose(m.bank[6 + i % 2][:, h * 256 + mt * 128:h * 256 + (mt + 1) * 128],
                                                   kv[l][:, mt, (2 * hp + h) * 128:(2 * hp + h + 1) * 128], m.ident[:, :])
                last.then_inc(ktr, 1)


def input_norm_phase(nc, m, sem, A):
    ldx = [sem(f"in_ldx{i}") for i in range(2)]
    ss, x2, tr, hev, ch = (sem("in_" + s) for s in ("ss", "x2", "tr", "hev", "ch"))
    V0 = m.V0
    x = [m.at(f"in_x{i}", [128, D], m.WS + 4096 * i) for i in range(2)]
    y = [m.at(f"in_y{i}", [128, D], m.WS + 8192 + 4096 * i) for i in range(2)]
    st = m.stat
    rows = lambda t: 128 if t < TT else NS
    with nc.Block() as block:
        @block.sync
        def _(s):
            for t in range(TT + 1):
                if t >= 2:
                    s.wait_ge(x2, t - 1)
                n = rows(t)
                src = A["x_prompt"][0, t * 128:(t + 1) * 128, :] if t < TT else A["x_sample"].rearrange("b s d -> (b s) d")
                s.dma_start(x[t % 2][0:n, :], src).then_inc(ldx[t % 2], 16)

        @block.scalar
        def _(act):
            for t in range(TT + 2):
                if t <= TT:
                    n, p = rows(t), t % 2
                    act.wait_ge(ldx[p], 16 * (t // 2 + 1))
                    if t >= 2:
                        act.wait_ge(tr, t - 1)
                    nc.scalar.activation(y[p][0:n, :], x[p][0:n, :], ACT.Square, accum_out=st[0:n, p:p + 1]).then_inc(ss, 1)
                    act.wait_ge(ss, 2 * t + 1)
                    nc.scalar.activation(st[0:n, 2 + p:3 + p], st[0:n, p:p + 1], ACT.Sqrt, bias=m.eps[0:n, :], scale=1.0 / D).then_inc(ss, 1)
                if t >= 1:
                    u, n = t - 1, rows(t - 1)
                    act.wait_ge(tr, u + 1)
                    for h in range(2):
                        i = nc.scalar.activation(m.hn[:, 4 * h:4 * h + 4, u * 128:u * 128 + n],
                                                 m.bank[2 * (u % 2) + h][:, :].rearrange("p (k c) -> p k c", k=4)[:, :, 0:n], ACT.Copy)
                    i.then_inc(hev, 1)

        @block.vector
        def _(v):
            c = Chain(v, ch)
            for t in range(TT + 1):
                n, p = rows(t), t % 2
                v.wait_ge(ss, 2 * t + 2)
                c.link(nc.vector.reciprocal(st[0:n, 4 + p:5 + p], st[0:n, 2 + p:3 + p]))
                nc.vector.tensor_scalar(y[p][0:n, :], x[p][0:n, :], st[0:n, 4 + p:5 + p], None, ALU.mult).then_inc(x2, 1)

        @block.tensor
        def _(pe):
            for t in range(TT + 1):
                n = rows(t)
                pe.wait_ge(x2, t + 1)
                if t >= 2:
                    pe.wait_ge(hev, t - 1)
                for k in range(KT):
                    last = nc.tensor.transpose(m.bank[2 * (t % 2) + k // 4][:, (k % 4) * 128:(k % 4) * 128 + n],
                                               y[t % 2][0:n, k * 128:(k + 1) * 128], m.ident[0:n, 0:n])
                last.then_inc(tr, 1)


def split_phase(nc, m, sem, l):
    hi = sem(f"sp_hi{l}")
    with nc.Block() as block:
        @block.scalar
        def _(act):
            for k in range(KT):
                nc.scalar.activation(m.hn_hi[:, k, :], m.hn[:, k, :], ACT.Copy, scale=m.prm[:, k, R_G + l:R_G + l + 1]).then_inc(hi, 1)

        @block.vector
        def _(v):
            for k in range(KT):
                v.wait_ge(hi, k + 1)
                nc.vector.scalar_tensor_tensor(m.hn_lo[:, k, :], m.hn[:, k, :], m.prm[:, k, R_G + l:R_G + l + 1],
                                               m.hn_hi[:, k, :].bitcast(F32), ALU.mult, ALU.subtract)


def item_phase(nc, m, sem, l, A):
    P = f"it{l}_"
    loaded = [sem(P + f"w_loaded{p}") for p in range(2)]
    names = ("w_hi w_lo b_done g_done b_free g_free kv_ld s_done m_ready e_done p_ready t_done pta_ready "
             "ptv_ready o_done z_ready gz_free mch chn ach swap cs_ld q_ready d_ready es_done uc_ready ri_done "
             "q2_ready sq_ready a_ready ip_ready n_done n_free vh_ready").split()
    S = {n: sem(P + n) for n in names}
    stored = [sem(P + f"stored{p}") for p in range(2)]
    row_stored = [sem(P + f"row_stored{p}") for p in range(2)]
    bd_ld = [sem(P + f"bd_ld{p}") for p in range(2)]
    PB, PG, S0, S1, S2, S3, T0, T1 = m.bank
    banks_s = [S2, S3, S0, S1] if l == 1 else [S0, S1]

    off = [m.V0]

    def buf(name, shape, dt=F32):
        t = m.at(P + name, shape, off[0], dt)
        off[0] += m.size(shape)
        return t

    gth, gh = buf("gth", [128, CH]), buf("gh", [128, CH])
    gz = [buf(f"gz{i}", [128, CH]) for i in range(2)]
    if l == 0:
        start = off[0]
        u_sb = buf("u_sb", [128, 3 + T])
        uc = buf("uc", [128, CH])
        qT = m.at(P + "qT", [128, CH], start + 8224)
        thr, thi, tt_, m1, a2, q2 = (buf(n, [128, CH]) for n in ("thr", "thi", "tt", "m1", "a2", "q2"))
        vh = [m.at(P + f"vh{i}", [128, 2, 128], start + 10272 + 1024 * i) for i in range(2)]
        aa = [buf(f"aa{i}", [128, CH]) for i in range(2)]
        hh = [buf(f"hh{i}", [128, CH]) for i in range(2)]
        bd = [[buf(f"bd{p}{g}", [128, 128]) for g in range(2)] for p in range(2)]
        Pm = m.at(P + "Pm", [128, 4, M], start)
        PTm = m.at(P + "PTm", [128, 2, CH], start + 4096)
        kmt, vm = buf("kmt", [128, NMH, M]), buf("vm", [128, 2, DMEM])
    else:
        kT, kV = m.kT, m.kV
        off[0] = m.kv_end
        qraw, qrot, cs, qf = buf("qraw", [128, CH]), buf("qrot", [128, CH]), buf("cs", [128, 2, CH]), buf("qf", [128, CH])
        p0 = off[0]
        Ps = buf("Ps", [128, 2, 4, 2 * W])
        PTs = buf("PTs", [128, 2, 2, CH])
        sk = [buf(f"sk{i}", [128, 2]) for i in range(2)]
        qT = m.at(P + "qT", [128, CH], m.kv_end)
        vh = [m.at(P + f"vh{i}", [128, 2, 128], m.kv_end + 2048 + 1024 * i) for i in range(2)]
        Pm, kmt = m.at(P + "Pm", [128, 4, M], p0), m.at(P + "kmt", [128, NMH, M], p0 + 4096)
        PTm, vm = m.at(P + "PTm", [128, 2, CH], p0 + 8192), m.at(P + "vm", [128, 2, DMEM], p0 + 12288)
    row = [m.srow_st[p] for p in range(2)]
    mx, negm, rs, rinv, es = (m.stat[:, 8 * i:8 * i + 8] for i in range(5))
    sden = m.stat[:, 40:48]
    w_in = A["w_in"][l].rearrange("(k p) n -> p k n", p=128)
    row_bank = {"mem": S3, "main": S3 if l == 0 else PB}
    NP = (NI - NMH) // 2

    first = {"mem": 0, "main": NMH}

    def item(kind, i, p):
        return 2 * i + p + first[kind]

    def chunk(kind, i, p, c):
        return 8 * i + 4 * p + c + NCH * first[kind]

    def before(i, p, c, n=1):
        q = 4 * p + c - n
        if q >= 0:
            return i, q // 4, q % 4
        return None if isinstance(i, int) and i == 0 else (i - 1, (q + 8) // 4, (q + 8) % 4)

    def cols(kind, j):
        if kind == "mem":
            return [[(2048 + 128 * j, 128, 0)], [(2560 + 128 * j, 128, 0)]]
        if l == 0:
            return [[(128 * j, 128, 0)], [(1024 + 128 * j, 128, 0)]]
        return [[(64 * j, 64, 0), (512 + 64 * j, 64, 64)], [(1024 + 64 * j, 64, 0), (1536 + 64 * j, 64, 64)]]

    main_inc = 32 if l == 0 else 64

    def load_w(s, kind, i, p):
        j = 2 * i + p
        for b, pieces in enumerate(cols(kind, j)):
            for c0, n, o in pieces:
                s.dma_start(m.w_raw[p][:, :, b, o:o + n], w_in[:, :, ds(c0, n)]).then_inc(loaded[p], 16)
        if l == 0 and kind == "main":
            for g, w in enumerate(("lru_wa", "lru_wx")):
                for r in range(2):
                    s.dma_start(bd[p][g][64 * r:64 * r + 64, 64 * r:64 * r + 64],
                                A[w][0].rearrange("n c d -> (n c) d")[ds(128 * j + 64 * r, 64), :]).then_inc(bd_ld[p], 16)

    def split_act(act, kind, i, p):
        act.wait_ge(loaded[p], 32 * (i + 1) if kind == "mem" else 64 + main_inc * (i + 1))
        nc.scalar.activation(m.w_hi[p][:, :, :, :], m.w_raw[p][:, :, :, :], ACT.Copy).then_inc(S["w_hi"], 1)

    def split_dve(v, kind, i, p):
        v.wait_ge(S["w_hi"], item(kind, i, p) + 1)
        nc.vector.tensor_tensor(m.w_lo[p][:, :, :, :], m.w_raw[p][:, :, :, :], m.w_hi[p][:, :, :, :].bitcast(F32),
                                ALU.subtract).then_inc(S["w_lo"], 1)

    def next_item(kind, i, p, last):
        if p == 0:
            return kind, i, 1
        if not last:
            return kind, i + 1, 0
        return ("main", 0, 0) if kind == "mem" else None

    def project(pe, kind, i, p, b, c):
        ps = (PB, PG)[b]
        if b == 0 and c == 0:
            pe.wait_ge(S["w_lo"], item(kind, i, p) + 1)
            if row_bank[kind] is PB:
                pe.wait_ge(S["n_free"], item(kind, i, p) + 1)
        pe.wait_ge(S["b_free" if b == 0 else "g_free"], chunk(kind, i, p, c) + 1)
        for k in range(KT):
            a, al = m.w_hi[p][:, k, b, :], m.w_lo[p][:, k, b, :]
            x, xl = m.hn_hi[:, k, c * CH:(c + 1) * CH], m.hn_lo[:, k, c * CH:(c + 1) * CH]
            for q, (s_, r_) in enumerate(((a, x), (a, xl), (al, x))):
                last = nc.tensor.matmul(ps[:, :], s_, r_, start=(k == 0 and q == 0), stop=(k == KT - 1 and q == 2))
        last.then_inc(S["b_done" if b == 0 else "g_done"], 1)

    def project_samples(pe, kind, i, p):
        ps = row_bank[kind]
        if ps is PB:
            pe.wait_ge(S["b_free"], chunk(kind, i, p, NCH - 1) + 2)
        else:
            pe.wait_ge(S["n_free"], item(kind, i, p) + 1)
        for k in range(KT):
            x, xl = m.hn_hi[:, k, T:TA], m.hn_lo[:, k, T:TA]
            w, wl = (t[p][:, k, :, :].rearrange("p b n -> p (b n)") for t in (m.w_hi, m.w_lo))
            for q, (s_, r_) in enumerate(((x, w), (xl, w), (x, wl))):
                last = nc.tensor.matmul(ps[0:NS, 0:256], s_, r_, start=(k == 0 and q == 0), stop=(k == KT - 1 and q == 2))
        last.then_inc(S["n_done"], 1)

    def evac_samples(act, kind, i, p):
        act.wait_ge(row_stored[p], 16 * (i + first[kind] // 2) + 16)
        act.wait_ge(S["n_done"], item(kind, i, p) + 1)
        nc.scalar.activation(row[p][0:NS, :], row_bank[kind][0:NS, 0:256], ACT.Copy).then_inc(S["n_free"], 1)

    def store_samples(s, kind, i, p):
        s.wait_ge(S["n_free"], item(kind, i, p) + 2)
        s.dma_start(m.srow_d[:, ds(256 * item(kind, i, p), 256)], row[p][0:NS, :]).then_inc(row_stored[p], 16)

    def evac_gate(act, kind, i, p, c):
        act.wait_ge(S["g_done"], chunk(kind, i, p, c) + 1)
        act.wait_ge(S["gz_free"], chunk(kind, i, p, c) + 1)
        nc.scalar.activation(gh[:, :], PG[:, :], ACT.Copy, scale=0.5)
        nc.scalar.activation(gth[:, :], PG[:, :], ACT.Tanh, scale=0.5).then_inc(S["g_free"], 1)

    def evac_branch(act, kind, i, p, c, dst):
        act.wait_ge(S["b_done"], chunk(kind, i, p, c) + 1)
        nc.scalar.activation(dst, PB[:, :], ACT.Copy).then_inc(S["b_free"], 1)

    def gate_product(v, kind, i, p, c):
        v.wait_ge(S["g_free"], chunk(kind, i, p, c) + 2)
        v.wait_ge(stored[c % 2], 64 * i + 32 * p + 32 * first[kind] + 16 * (c // 2) + 16)
        nc.vector.scalar_tensor_tensor(gz[c % 2][:, :], gth[:, :], 1.0, gh[:, :], ALU.add, ALU.mult).then_inc(S["gz_free"], 1)

    def gate_result(v, kind, i, p, c, y):
        v.wait_ge(S["gz_free"], chunk(kind, i, p, c) + 2)
        nc.vector.tensor_tensor(gz[c % 2][:, :], gz[c % 2][:, :], y, ALU.mult).then_inc(S["z_ready"], 1)

    def store_z(s, kind, i, p, c):
        s.wait_ge(S["z_ready"], chunk(kind, i, p, c) + 1)
        s.dma_start(m.z_d[ds(item(kind, i, p), 1), :, c * CH:(c + 1) * CH].rearrange("a p t -> p (a t)"), gz[c % 2][:, :]).then_inc(stored[c % 2], 16)

    def mem_flip(pe, i, p, c):
        pe.wait_ge(S["p_ready"], chunk("mem", i, p, c) + 1)
        for mt in range(2):
            for t in range(4):
                last = nc.tensor.transpose((T0, T1)[mt][:, t * 128:(t + 1) * 128], Pm[:, t, mt * 128:(mt + 1) * 128], m.ident[:, :])
        last.then_inc(S["t_done"], 1)

    def mem_values(pe, i, p, c):
        pe.wait_ge(S["pta_ready"], chunk("mem", i, p, c) + 1)
        pe.wait_ge(S["ptv_ready"], chunk("mem", i, p, c) + 1)
        for mt in range(2):
            last = nc.tensor.matmul(S2[:, :], vh[p][:, mt, :], PTm[:, mt, :], start=(mt == 0), stop=(mt == 1))
        last.then_inc(S["o_done"], 1)

    def mem_scores(pe, i, p, c):
        pe.wait_ge(S["kv_ld"], 32)
        pe.wait_ge(S["b_free"], chunk("mem", i, p, c) + 2)
        for t in range(4):
            last = nc.tensor.matmul((S0, S1)[t // 2][:, (t % 2) * M:(t % 2 + 1) * M], qT[:, t * 128:(t + 1) * 128],
                                    kmt[:, 2 * i + p, :], start=True, stop=True)
        last.then_inc(S["s_done"], 1)

    def mem_exp(act, i, p, c):
        act.wait_ge(S["m_ready"], chunk("mem", i, p, c) + 1)
        for t in range(4):
            nc.scalar.activation(Pm[:, t, :], (S0, S1)[t // 2][:, (t % 2) * M:(t % 2 + 1) * M], ACT.Exp,
                                 bias=negm[:, t:t + 1], scale=MEM_SCALE, accum_out=rs[:, t:t + 1]).then_inc(S["e_done"], 1)

    def mem_flip_act(act, i, p, c):
        act.wait_ge(S["t_done"], chunk("mem", i, p, c) + 1)
        nc.scalar.activation(PTm[:, 0, :], T0[:, :], ACT.Copy).then_inc(S["pta_ready"], 1)

    def mem_flip_dve(v, i, p, c):
        v.wait_ge(S["t_done"], chunk("mem", i, p, c) + 1)
        nc.vector.tensor_copy(PTm[:, 1, :], T1[:, :]).then_inc(S["ptv_ready"], 1)

    def mem_max(v, chn, i, p, c):
        v.wait_ge(S["s_done"], chunk("mem", i, p, c) + 1)
        for b in range(2):
            r = nc.vector.reduce_max(mx[:, 2 * b:2 * b + 2], (S0, S1)[b][:, :].rearrange("p (t k) -> p t k", t=2), AX_X)
        chn.link(r)
        nc.vector.tensor_scalar(negm[:, 0:4], mx[:, 0:4], -MEM_SCALE, None, ALU.mult).then_inc(S["m_ready"], 1)

    def mem_norm(v, chn, i, p, c):
        v.wait_ge(S["e_done"], 4 * (chunk("mem", i, p, c) + 1))
        chn.link(nc.vector.reciprocal(rinv[:, 0:4], rs[:, 0:4]))
        for t in range(4):
            r = nc.vector.tensor_scalar(Pm[:, t, :], Pm[:, t, :], rinv[:, t:t + 1], None, ALU.mult)
        r.then_inc(S["p_ready"], 1)

    def mem_result(v, i, p, c):
        v.wait_ge(S["o_done"], chunk("mem", i, p, c) + 1)
        gate_result(v, "mem", i, p, c, S2[:, :])

    def mem_pe(pe, i, p, last):
        for c in range(NCH):
            b = before(i, p, c)
            project(pe, "mem", i, p, 0, c)
            project(pe, "mem", i, p, 1, c)
            if b:
                mem_flip(pe, *b)
            mem_scores(pe, i, p, c)
            if b:
                mem_values(pe, *b)
        project_samples(pe, "mem", i, p)
        if last and p:
            mem_flip(pe, i, p, NCH - 1)
            mem_values(pe, i, p, NCH - 1)

    def mem_act(act, i, p, last):
        for c in range(NCH):
            b = before(i, p, c)
            if b:
                mem_exp(act, *b)
            evac_branch(act, "mem", i, p, c, qT[:, :])
            evac_gate(act, "mem", i, p, c)
            if b:
                mem_flip_act(act, *b)
            if c == 1:
                split_act(act, *next_item("mem", i, p, last))
        evac_samples(act, "mem", i, p)
        if last and p:
            mem_exp(act, i, p, NCH - 1)
            mem_flip_act(act, i, p, NCH - 1)

    def mem_dve(v, i, p, last):
        n = 8 if not (last and p) else 10
        chn = Chain(v, S["mch"], (2 * i + p) * 8 - (2 if not (i == 0 and p == 0) else 0))
        if i == 0 and p == 0:
            v.wait_ge(S["kv_ld"], 32)
        nc.vector.tensor_copy(vh[p][:, :, :], vm[:, :, (2 * i + p) * 128:(2 * i + p + 1) * 128])
        for c in range(NCH):
            b, b2 = before(i, p, c), before(i, p, c, 2)
            if b:
                mem_max(v, chn, *b)
            if b2:
                mem_result(v, *b2)
            if b:
                gate_product(v, "mem", *b)
                mem_norm(v, chn, *b)
            if c == 1:
                split_dve(v, *next_item("mem", i, p, last))
            if b:
                mem_flip_dve(v, *b)
        if last and p:
            mem_max(v, chn, i, p, NCH - 1)
            mem_result(v, i, p, NCH - 2)
            gate_product(v, "mem", i, p, NCH - 1)
            mem_norm(v, chn, i, p, NCH - 1)
            mem_flip_dve(v, i, p, NCH - 1)
            mem_result(v, i, p, NCH - 1)

    def lru_pe(pe, i, p, last):
        for c in range(NCH):
            project(pe, "main", i, p, 0, c)
            project(pe, "main", i, p, 1, c)
            if c == 0:
                pe.wait_ge(bd_ld[p], 64 * (i + 1))
            pe.wait_ge(S["uc_ready"], 8 * i + 4 * p + c + 1)
            nc.tensor.matmul(S0[:, :], bd[p][0][:, :], uc[:, :], start=True, stop=True)
            nc.tensor.matmul(S1[:, :], bd[p][1][:, :], uc[:, :], start=True, stop=True).then_inc(S["ri_done"], 1)
        project_samples(pe, "main", i, p)

    def lru_sqrt(act, i, p, c):
        act.wait_ge(S["q2_ready"], 8 * i + 4 * p + c + 1)
        nc.scalar.activation(q2[:, :], q2[:, :], ACT.Sqrt, scale=0.25).then_inc(S["sq_ready"], 1)

    def lru_act(act, i, p, last):
        par = m.lru_par
        chn = Chain(act, S["ach"], (2 * i + p) * 5)
        for c in range(NCH):
            b = before(i, p, c)
            if b and c == 0:
                act.wait_ge(S["a_ready"], 8 * i + 4 * p)
            evac_branch(act, "main", i, p, c, u_sb[:, 3 + c * CH:3 + (c + 1) * CH])
            if c == 0:
                chn.link(nc.scalar.activation(par[:, :], m.dvp[:, ds(2 * i + p, 1), :].rearrange("p a j -> p (a j)"), ACT.Copy))
            if b:
                lru_sqrt(act, *b)
            evac_gate(act, "main", i, p, c)
            if c == 1 and next_item("main", i, p, last):
                split_act(act, *next_item("main", i, p, last))
            act.wait_ge(S["ri_done"], 8 * i + 4 * p + c + 1)
            nc.scalar.activation(thi[:, :], S1[:, :], ACT.Tanh, bias=par[:, 3:4], scale=0.5)
            chn.link(nc.scalar.activation(thr[:, :], S0[:, :], ACT.Tanh, bias=par[:, 2:3], scale=0.5))
            nc.scalar.activation(aa[c % 2][:, :], thr[:, :], ACT.Exp, bias=par[:, 0:1], scale=par[:, 0:1])
            nc.scalar.activation(tt_[:, :], thr[:, :], ACT.Tanh, bias=par[:, 1:2], scale=par[:, 1:2]).then_inc(S["a_ready"], 1)
        evac_samples(act, "main", i, p)
        if last and p:
            lru_sqrt(act, i, p, NCH - 1)
        assert chn.n == 5

    def lru_scan(v, chn, i, p, c):
        v.wait_ge(S["sq_ready"], 8 * i + 4 * p + c + 1)
        chn.link(nc.vector.tensor_tensor(m1[:, :], m1[:, :], q2[:, :], ALU.mult))
        init = 0.0 if c == 0 else hh[(c + 1) % 2][:, CH - 1:CH]
        chn.link(nc.vector.tensor_tensor_scan(hh[c % 2][:, :], aa[c % 2][:, :], m1[:, :], init, ALU.mult, ALU.add))
        gate_product(v, "main", i, p, c)
        gate_result(v, "main", i, p, c, hh[c % 2][:, :])
        if c == NCH - 1:
            nc.vector.tensor_copy(m.out_t[:, ds(2 * i + p, 1), 0], hh[c % 2][:, CH - 1:CH])

    def lru_dve(v, i, p, last):
        f, CHN = 2 * i + p, 6 * NCH
        begin = isinstance(i, int) and i == 0 and p == 0
        chn = Chain(v, S["chn"], f * CHN - (0 if begin else 2))
        pr = lambda j: m.prm[:, ds(f, 1), j]
        for c in range(NCH):
            b = before(i, p, c)
            v.wait_ge(S["b_free"], chunk("main", i, p, c) + 2)
            u = lambda k: u_sb[:, c * CH + k:c * CH + k + CH]
            chn.link(nc.vector.tensor_scalar(uc[:, :], u(0), pr(R_CW), pr(R_CB), ALU.mult, ALU.add))
            chn.link(nc.vector.scalar_tensor_tensor(uc[:, :], u(1), pr(R_CW + 1), uc[:, :], ALU.mult, ALU.add))
            chn.link(nc.vector.scalar_tensor_tensor(uc[:, :], u(2), pr(R_CW + 2), uc[:, :], ALU.mult, ALU.add))
            nc.vector.scalar_tensor_tensor(uc[:, :], u(3), pr(R_CW + 3), uc[:, :], ALU.mult, ALU.add).then_inc(S["uc_ready"], 1)
            if c == NCH - 1:
                nc.vector.tensor_copy(m.out_t[:, ds(f, 1), 1:4].rearrange("p a k -> p (a k)"), u_sb[:, T:T + 3])
            if b:
                lru_scan(v, chn, *b)
            v.wait_ge(S["a_ready"], 8 * i + 4 * p + c + 1)
            v.wait_ge(S["uc_ready"], 8 * i + 4 * p + c + 1)
            nc.vector.scalar_tensor_tensor(m1[:, :], thi[:, :], 1.0, uc[:, :], ALU.add, ALU.mult)
            chn.link(nc.vector.tensor_tensor(a2[:, :], aa[c % 2][:, :], aa[c % 2][:, :], ALU.mult))
            nc.vector.scalar_tensor_tensor(q2[:, :], a2[:, :], 1.0, tt_[:, :], ALU.add, ALU.mult).then_inc(S["q2_ready"], 1)
            if c == 1 and next_item("main", i, p, last):
                split_dve(v, *next_item("main", i, p, last))
        if last and p:
            lru_scan(v, chn, i, p, NCH - 1)
        assert chn.n == CHN - (2 if begin else 0) + (2 if last and p else 0)

    flip_banks = ((T0, T1), (S0, S1))

    def swa_flip(pe, i, p, c):
        pe.wait_ge(S["p_ready"], chunk("main", i, p, c) + 1)
        for h in range(2):
            for kt in range(2):
                for t in range(4):
                    last = nc.tensor.transpose(flip_banks[h][kt][:, t * 128:(t + 1) * 128], Ps[:, h, t, kt * 128:(kt + 1) * 128], m.ident[:, :])
        last.then_inc(S["t_done"], 1)

    def swa_scores(pe, i, p, c, h):
        if h == 0:
            pe.wait_ge(S["q_ready"], 8 * i + 4 * p + c + 1)
        for t in range(4):
            last = nc.tensor.matmul(banks_s[2 * h + t // 2][:, (t % 2) * 256:(t % 2 + 1) * 256],
                                    qf[64 * h:64 * h + 64, t * 128:(t + 1) * 128],
                                    kT[64 * h:64 * h + 64, (4 * c + t) * 128:(4 * c + t + 2) * 128], start=True, stop=True)
        last.then_inc(S["s_done"], 1)

    def swa_values(pe, i, p, c):
        for t in range(4):
            for h in range(2):
                for kt in range(2):
                    last = nc.tensor.matmul(T0[64 * h:64 * h + 64, t * 128:(t + 1) * 128], kV[:, 4 * c + t + kt, 64 * h:64 * h + 64],
                                            PTs[:, h, kt, t * 128:(t + 1) * 128], start=(kt == 0), stop=(kt == 1))
        last.then_inc(S["o_done"], 1)

    def swa_pe(pe, i, p, last):
        for c in range(NCH):
            b = before(i, p, c)
            project(pe, "main", i, p, 0, c)
            project(pe, "main", i, p, 1, c)
            if b:
                swa_flip(pe, *b)
            swa_scores(pe, i, p, c, 0)
            if b:
                pe.wait_ge(S["pta_ready"], chunk("main", *b) + 1)
                pe.wait_ge(S["ptv_ready"], chunk("main", *b) + 1)
            swa_scores(pe, i, p, c, 1)
            if c == NCH - 1:
                project_samples(pe, "main", i, p)
            if b:
                swa_values(pe, *b)
        if last and p:
            swa_flip(pe, i, p, NCH - 1)
            pe.wait_ge(S["pta_ready"], chunk("main", i, p, NCH))
            pe.wait_ge(S["ptv_ready"], chunk("main", i, p, NCH))
            swa_values(pe, i, p, NCH - 1)

    def swa_exp(act, i, p, c, h):
        q = 8 * i + 4 * p + c
        act.wait_ge(S["m_ready"], 16 + 2 * q + h + 1)
        for t in range(4):
            j = 4 * h + t
            nc.scalar.activation(Ps[:, h, t, :], Ps[:, h, t, :], ACT.Exp, bias=negm[:, j:j + 1],
                                 accum_out=rs[:, j:j + 1]).then_inc(S["e_done"], 1)
        if h:
            act.wait_ge(S["d_ready"], q + 1)
            nc.scalar.activation(es[:, :], es[:, :], ACT.Exp).then_inc(S["es_done"], 1)

    def swa_flip_act(act, i, p, c):
        act.wait_ge(S["t_done"], chunk("main", i, p, c) + 1)
        nc.scalar.activation(PTs[:, 0, 0, :], T0[:, :], ACT.Copy)
        nc.scalar.activation(PTs[:, 1, 0, :], S0[:, :], ACT.Copy).then_inc(S["pta_ready"], 1)

    def swa_act(act, i, p, last):
        for c in range(NCH):
            b = before(i, p, c)
            if b:
                swa_exp(act, *b, 0)
                swa_exp(act, *b, 1)
            evac_branch(act, "main", i, p, c, qraw[:, :])
            evac_gate(act, "main", i, p, c)
            if b:
                swa_flip_act(act, *b)
            if c == 1 and next_item("main", i, p, last):
                split_act(act, *next_item("main", i, p, last))
        evac_samples(act, "main", i, p)
        if last and p:
            swa_exp(act, i, p, NCH - 1, 0)
            swa_exp(act, i, p, NCH - 1, 1)
            swa_flip_act(act, i, p, NCH - 1)

    def swa_max(v, chn, i, p, c):
        q = 8 * i + 4 * p + c
        for h in range(2):
            v.wait_ge(S["s_done"], 16 + 2 * q + h + 1)
            nc.vector.memset(m.stat[:, 48 + h:49 + h], 0.0)
            for t in range(4):
                j = 4 * h + t
                mk = m.mask[:, 0:3:2, :] if c == 0 and t == 0 else m.mask[:, 1:3, :]
                sc = banks_s[2 * h + t // 2][:, (t % 2) * 256:(t % 2 + 1) * 256].rearrange("p (a k) -> p a k", a=2)
                r = nc.vector.tensor_tensor_reduce(out=Ps[:, h, t, :].rearrange("p (a k) -> p a k", a=2), in0=sc, in1=mk, scale=1.0,
                                                   scalar=sk[p][:, h:h + 1], op0=ALU.add, op1=ALU.max, accum_out=mx[:, j:j + 1])
            chn.link(r)
            nc.vector.tensor_scalar(negm[:, 4 * h:4 * h + 4], mx[:, 4 * h:4 * h + 4], -1.0, None, ALU.mult).then_inc(S["m_ready"], 1)
        v.wait_ge(S["m_ready"], 16 + 2 * (q + 1))
        nc.vector.tensor_tensor(es[:, :].rearrange("p (h t) -> p h t", h=2), negm[:, :].rearrange("p (h t) -> p h t", h=2),
                                bc(sk[p][:, :], 4), ALU.add).then_inc(S["d_ready"], 1)

    def swa_norm(v, chn, i, p, c):
        q = 8 * i + 4 * p + c
        v.wait_ge(S["e_done"], 64 + 8 * (q + 1))
        v.wait_ge(S["es_done"], q + 1)
        chn.link(nc.vector.tensor_tensor(sden, rs[:, :], es[:, :], ALU.add))
        chn.link(nc.vector.reciprocal(rinv[:, :], sden))
        for j in range(8):
            pj = Ps[:, j // 4, j % 4, :]
            r = nc.vector.tensor_scalar(pj, pj, rinv[:, j:j + 1], None, ALU.mult)
        r.then_inc(S["p_ready"], 1)

    def swa_rope(v, chn, i, p, c):
        q = 8 * i + 4 * p + c
        v.wait_ge(S["swap"], 64 * (q + 1))
        v.wait_ge(S["cs_ld"], 16 * (q + 1))
        nc.vector.tensor_tensor(qraw[:, :], qraw[:, :], cs[:, 0, :], ALU.mult)
        chn.link(nc.vector.tensor_tensor(qrot[:, :], qrot[:, :], cs[:, 1, :], ALU.mult))
        nc.vector.tensor_tensor(qf[:, :], qraw[:, :], qrot[:, :], ALU.add).then_inc(S["q_ready"], 1)

    def swa_flip_dve(v, i, p, c):
        v.wait_ge(S["t_done"], chunk("main", i, p, c) + 1)
        nc.vector.tensor_copy(PTs[:, 0, 1, :], T1[:, :])
        nc.vector.tensor_copy(PTs[:, 1, 1, :], S1[:, :]).then_inc(S["ptv_ready"], 1)

    def swa_result(v, i, p, c):
        v.wait_ge(S["o_done"], chunk("main", i, p, c) + 1)
        gate_result(v, "main", i, p, c, T0[:, :])

    def swa_dve(v, i, p, last):
        f = 2 * i + p
        CHN = 1 + 5 * NCH
        begin = isinstance(i, int) and i == 0 and p == 0
        chn = Chain(v, S["chn"], f * CHN - (0 if begin else 4))
        nc.vector.tensor_copy(sk[p][:, 0:1], m.sink_bc[:, ds(f, 1)])
        chn.link(nc.vector.tensor_copy(sk[p][:, 1:2], m.sink_bc[:, ds(8 + f, 1)]))
        for c in range(NCH):
            b, b2 = before(i, p, c), before(i, p, c, 2)
            if b:
                swa_max(v, chn, *b)
            if b2:
                swa_result(v, *b2)
            if b:
                gate_product(v, "main", *b)
                swa_norm(v, chn, *b)
            swa_rope(v, chn, i, p, c)
            if c == 1 and next_item("main", i, p, last):
                split_dve(v, *next_item("main", i, p, last))
            if b:
                swa_flip_dve(v, *b)
        if last and p:
            swa_max(v, chn, i, p, NCH - 1)
            swa_result(v, i, p, NCH - 2)
            gate_product(v, "main", i, p, NCH - 1)
            swa_norm(v, chn, i, p, NCH - 1)
            swa_flip_dve(v, i, p, NCH - 1)
            swa_result(v, i, p, NCH - 1)
        assert chn.n == CHN - (4 if begin else 0) + (4 if last and p else 0), chn.n

    def item_sp(s, kind, i, p, last):
        nxt = next_item(kind, i, p, last)
        if nxt:
            if not (kind == "mem" and i == 0 and p == 0):
                s.wait_ge(S["n_done"], item(kind, i, p))
            load_w(s, *nxt)
        lag = 1 if kind == "main" and l == 0 else 2
        for c in range(NCH):
            if l == 1 and kind == "main":
                s.wait_ge(S["b_free"], chunk(kind, i, p, c) + 2)
                for r in range(4):
                    s.dma_start(qrot[32 * r:32 * r + 32, :], qraw[32 * (r ^ 1):32 * (r ^ 1) + 32, :]).then_inc(S["swap"], 16)
                s.dma_start(cs[:, :, :], A["rope_q"][:, :, c * CH:(c + 1) * CH]).then_inc(S["cs_ld"], 16)
            b = before(i, p, c, lag)
            if b:
                store_z(s, kind, *b)
        store_samples(s, kind, i, p)
        if last and p:
            for c in range(NCH - lag, NCH):
                store_z(s, kind, i, p, c)

    def both(f, i, last=False):
        for p in range(2):
            f(i, p, last)

    def engine_loop(eng, mem_item, main_item):
        both(mem_item, 0)
        both(mem_item, 1, True)
        eng.wait_ge(S["o_done"], NMH * NCH)
        if l == 0:
            eng.wait_ge(S["ip_ready"], 3)
        both(main_item, 0)
        with eng.Fori(1, NP - 1) as i:
            both(main_item, i)
        both(main_item, NP - 1, True)

    with nc.Block() as block:
        @block.sync
        def _(s):
            s.dma_start(kmt[:, :, :].rearrange("p h m -> p (h m)"), m.kmt_d[l]).then_inc(S["kv_ld"], 16)
            s.dma_start(vm[:, :, :], A["mem_v"][l, 0].rearrange("(t p) h d -> p t (h d)", p=128)).then_inc(S["kv_ld"], 16)
            for p in range(2):
                s.sem_inc(stored[p], 16)
                s.sem_inc(row_stored[p], 16)
            load_w(s, "mem", 0, 0)
            engine_loop(s, lambda i, p, last: item_sp(s, "mem", i, p, last), lambda i, p, last: item_sp(s, "main", i, p, last))
            for p in range(2):
                s.wait_ge(stored[p], 16 * (NI * NCH // 2 + 1))
                s.wait_ge(row_stored[p], 16 * (NI // 2 + 1))

        @block.gpsimd
        def _(g):
            if l == 0:
                for p in range(2):
                    for q in range(2):
                        for r in range(2):
                            last = g.memset(bd[p][q][64 * r:64 * r + 64, 64 * (1 - r):64 * (1 - r) + 64], 0.0)
                last.then_inc(S["ip_ready"], 1)
                g.wait_ge(S["ip_ready"], 1)
                g.wait_ge(S["o_done"], NMH * NCH)
                g.memset(u_sb[:, 0:3], 0.0).then_inc(S["ip_ready"], 2)

        @block.scalar
        def _(act):
            for n in ("b_free", "g_free", "n_free"):
                act.sem_inc(S[n], 1)
            split_act(act, "mem", 0, 0)
            engine_loop(act, lambda *a: mem_act(act, *a), lambda *a: (lru_act, swa_act)[l](act, *a))

        @block.vector
        def _(v):
            v.sem_inc(S["gz_free"], 1)
            split_dve(v, "mem", 0, 0)
            engine_loop(v, lambda *a: mem_dve(v, *a), lambda *a: (lru_dve, swa_dve)[l](v, *a))

        @block.tensor
        def _(pe):
            engine_loop(pe, lambda *a: mem_pe(pe, *a), lambda *a: (lru_pe, swa_pe)[l](pe, *a))


def sample_rows_phase(nc, m, sem, l):
    ld, tr = sem(f"sr{l}_ld"), sem(f"sr{l}_tr")
    rows = m.at(f"sr{l}_rows", [NS, 2 * CAT], m.LO)
    ps = m.bank[0][:, 0:2 * NI * NS].rearrange("p (n b s) -> p n b s", n=NI, b=2)
    with nc.Block() as block:
        @block.sync
        def _(s):
            s.dma_start(rows[:, :], m.srow_d).then_inc(ld, 16)

        @block.tensor
        def _(pe):
            pe.wait_ge(ld, 16)
            for n in range(NI):
                for b in range(2):
                    last = nc.tensor.transpose(ps[:, n, b, :], rows[:, 256 * n + 128 * b:256 * n + 128 * b + 128], m.ident[0:NS, 0:NS])
            last.then_inc(tr, 1)

        @block.scalar
        def _(act):
            act.wait_ge(tr, 1)
            nc.scalar.activation(m.bs[:, :, :], ps[:, :, 0, :], ACT.Copy)
            nc.scalar.activation(m.gh_s[:, :, :], ps[:, :, 1, :], ACT.Copy, scale=0.5)
            nc.scalar.activation(m.gth_s[:, :, :], ps[:, :, 1, :], ACT.Tanh, scale=0.5)


def sample_lru_phase(nc, m, sem, A, outs):
    ld, cp, ch, ga, mm, ex, sq, tr, ev, st = (sem("sl_" + s) for s in ("ld", "cp", "ch", "ga", "mm", "ex", "sq", "tr", "ev", "st"))
    zb = sem("sl_zb")
    H = m.HI
    n = KT * NS
    a = lambda name, k: m.at("sl_" + name, [128, KT, NS], H + 16384 + 256 * k)
    bd = m.at("sl_bd", [128, KT, 2, 128], H)
    uc, t1, thr, thi, ea, et, m1, a2, q2, h, gz = (a(s, k) for k, s in enumerate(("uc", "t1", "thr", "thi", "ea", "et", "m1", "a2", "q2", "h", "gz")))
    states = m.at("sl_rows", [20, D], H + 24576)
    R, I = (m.bank[b][:, 0:n].rearrange("p (k s) -> p k s", k=KT) for b in range(2))
    u = m.bs[:, NMH:NI, :]
    stt = m.prm[:, :, R_ST:R_ST + 24].rearrange("p k (s c) -> p k s c", c=3)
    col = lambda j: bc(m.prm[:, :, j], NS)
    dv = lambda j: bc(m.dvp[:, :, j], NS)
    with nc.Block() as block:
        @block.gpsimd
        def _(g):
            g.memset(bd[:, :, :, :], 0.0).then_inc(zb, 1)

        @block.sync
        def _(s):
            s.wait_ge(zb, 1)
            for q, w in enumerate(("lru_wa", "lru_wx")):
                for r in range(2):
                    s.dma_start(bd[64 * r:64 * r + 64, :, q, 64 * r:64 * r + 64],
                                A[w][0].rearrange("(k r) c d -> r c k d", r=2)[r]).then_inc(ld, 16)
            s.dma_start(outs["conv_s"][0, :, 0:2, :], A["state_conv"][0, :, 1:3, :]).then_inc(st, 16)
            s.wait_ge(ev, 1)
            s.dma_start(outs["lru_p"][0], states[0:1, :]).then_inc(st, 16)
            s.dma_start(outs["conv_p"][0, 0], states[1:4, :]).then_inc(st, 16)
            s.dma_start(outs["lru_s"][0], states[4:12, :]).then_inc(st, 16)
            s.dma_start(outs["conv_s"][0, :, 2, :], states[12:20, :]).then_inc(st, 16)
            s.wait_ge(st, 80)

        @block.tensor
        def _(pe):
            pe.wait_ge(ld, 64)
            pe.wait_ge(cp, 1)
            for k in range(KT):
                nc.tensor.matmul(R[:, k, :], bd[:, k, 0, :], uc[:, k, :], start=True, stop=True)
                last = nc.tensor.matmul(I[:, k, :], bd[:, k, 1, :], uc[:, k, :], start=True, stop=True)
            last.then_inc(mm, 1)
            pe.wait_ge(cp, 2)
            for k in range(KT):
                last = nc.tensor.transpose(m.bank[2 + k // 4][0:20, (k % 4) * 128:(k % 4 + 1) * 128], m.out_t[:, k, :], m.ident[:, :])
            last.then_inc(tr, 1)

        @block.scalar
        def _(act):
            act.wait_ge(ga, 2)
            nc.scalar.activation(thr[:, :, :], thr[:, :, :], ACT.Tanh, scale=0.5)
            nc.scalar.activation(thi[:, :, :], thi[:, :, :], ACT.Tanh, scale=0.5).then_inc(ex, 1)
            act.wait_ge(ga, 4)
            nc.scalar.activation(ea[:, :, :], ea[:, :, :], ACT.Exp)
            nc.scalar.activation(et[:, :, :], et[:, :, :], ACT.Tanh).then_inc(ex, 1)
            act.wait_ge(sq, 1)
            nc.scalar.activation(q2[:, :, :], q2[:, :, :], ACT.Sqrt, scale=0.25).then_inc(sq, 1)

        @block.vector
        def _(v):
            c = Chain(v, ch)
            tt = nc.vector.tensor_tensor
            c.link(tt(uc[:, :, :], u, col(R_CW + 3), ALU.mult))
            c.link(tt(uc[:, :, :], uc[:, :, :], col(R_CB), ALU.add))
            for k in range(3):
                c.link(tt(t1[:, :, :], stt[:, :, :, k], col(R_CW + k), ALU.mult))
                if k < 2:
                    c.link(tt(uc[:, :, :], uc[:, :, :], t1[:, :, :], ALU.add))
            tt(uc[:, :, :], uc[:, :, :], t1[:, :, :], ALU.add).then_inc(cp, 1)
            v.wait_ge(mm, 1)
            tt(thr[:, :, :], R, col(R_BA), ALU.add).then_inc(ga, 1)
            tt(thi[:, :, :], I, col(R_BX), ALU.add).then_inc(ga, 1)
            v.wait_ge(ex, 1)
            c.link(nc.vector.tensor_scalar(thr[:, :, :], thr[:, :, :], 1.0, None, ALU.add))
            tt(ea[:, :, :], thr[:, :, :], dv(0), ALU.mult).then_inc(ga, 1)
            tt(et[:, :, :], thr[:, :, :], dv(1), ALU.mult).then_inc(ga, 1)
            v.wait_ge(ex, 2)
            v.wait_ge(cp, 1)
            nc.vector.scalar_tensor_tensor(m1[:, :, :], thi[:, :, :], 1.0, uc[:, :, :], ALU.add, ALU.mult)
            c.link(tt(a2[:, :, :], ea[:, :, :], ea[:, :, :], ALU.mult))
            nc.vector.scalar_tensor_tensor(q2[:, :, :], a2[:, :, :], 1.0, et[:, :, :], ALU.add, ALU.mult).then_inc(sq, 1)
            c.link(tt(h[:, :, :], ea[:, :, :], m.prm[:, :, R_H0:R_H0 + 8], ALU.mult))
            v.wait_ge(sq, 2)
            c.link(tt(m1[:, :, :], m1[:, :, :], q2[:, :, :], ALU.mult))
            c.link(tt(h[:, :, :], h[:, :, :], m1[:, :, :], ALU.add))
            c.link(nc.vector.tensor_copy(m.out_t[:, :, 4:12], h[:, :, :]))
            nc.vector.tensor_copy(m.out_t[:, :, 12:20], u).then_inc(cp, 1)
            c.link(nc.vector.scalar_tensor_tensor(gz[:, :, :], m.gth_s[:, NMH:NI, :], 1.0, m.gh_s[:, NMH:NI, :], ALU.add, ALU.mult))
            tt(m.zs[:, NMH:NI, :], gz[:, :, :], h[:, :, :], ALU.mult)
            v.wait_ge(tr, 1)
            nc.vector.tensor_copy(states[0:20, 0:512], m.bank[2][0:20, :])
            c.link(nc.vector.tensor_copy(states[0:20, 512:1024], m.bank[3][0:20, :]))
            v.sem_inc(ev, 1)


def sample_mem_phase(nc, m, sem, l, A):
    P = f"sm{l}_"
    ldk, ldv = [sem(P + f"ldk{i}") for i in range(2)], sem(P + "ldv")
    kt_d, kt_e, s_d, s_e, t_d, m_r, e_d, p_r, pt_d, pt_e, o_d, ch = (sem(P + s) for s in
        ("kt_d", "kt_e", "s_d", "s_e", "t_d", "m_r", "e_d", "p_r", "pt_d", "pt_e", "o_d", "ch"))
    N = NMH * NS
    H = m.LO
    kb = [m.at(P + f"k{i}", [128, 2, DMEM], H + 4096 * i) for i in range(2)]
    kt = [m.at(P + f"kt{i}", [128, NMH, M], H + 8192 + 4096 * i) for i in range(2)]
    vb = m.at(P + "v", [128, NS, 2, DMEM], H + 16384)
    sT = m.at(P + "sT", [128, 2, N], H + 49152)
    pT = m.at(P + "pT", [128, 2, N], H + 49152 + 256)
    pr = m.at(P + "p", [N, M], H + 49152 + 512)
    gz = m.at(P + "gz", [128, NMH, NS], H + 49152 + 1536)
    st = m.at(P + "st", [N, 8], H + 49152 + 1664)
    b0, b1, b2, b3, b4 = m.bank[0], m.bank[1], m.bank[2], m.bank[3], m.bank[4]
    with nc.Block() as block:
        @block.sync
        def _(s):
            for b in range(NS):
                if b >= 2:
                    s.wait_ge(kt_d, b - 1)
                s.dma_start(kb[b % 2][:, :, :], A["cache_mem_k"][l, b].rearrange("(t p) h d -> p t (h d)", p=128)).then_inc(ldk[b % 2], 16)
                s.dma_start(vb[:, b, :, :], A["cache_mem_v"][l, b].rearrange("(t p) h d -> p t (h d)", p=128)).then_inc(ldv, 16)

        @block.tensor
        def _(pe):
            def scores(b):
                pe.wait_ge(kt_e, 2 * (b + 1))
                for h in range(NMH):
                    for t in range(2):
                        last = nc.tensor.matmul(b4[:, t * N + h * NS + b:t * N + h * NS + b + 1], kt[b % 2][:, h, t * 128:(t + 1) * 128],
                                                m.bs[:, h, b:b + 1], start=True, stop=True)
                last.then_inc(s_d, 1)

            for b in range(NS):
                pe.wait_ge(ldk[b % 2], 16 * (b // 2 + 1))
                if b >= 2:
                    pe.wait_ge(kt_e, 2 * (b - 1))
                for h in range(NMH):
                    for t in range(2):
                        last = nc.tensor.transpose(m.bank[2 * (b % 2) + h // 2][:, (h % 2) * M + t * 128:(h % 2) * M + (t + 1) * 128],
                                                   kb[b % 2][:, t, h * 128:(h + 1) * 128], m.ident[:, :])
                last.then_inc(kt_d, 1)
                if b:
                    scores(b - 1)
            scores(NS - 1)
            pe.wait_ge(s_e, 1)
            for t in range(2):
                last = nc.tensor.transpose(b0[0:N, t * 128:(t + 1) * 128], sT[:, t, :], m.ident[:, :])
            last.then_inc(t_d, 1)
            pe.wait_ge(p_r, 1)
            for t in range(2):
                last = nc.tensor.transpose(b1[:, t * N:(t + 1) * N], pr[:, t * 128:(t + 1) * 128], m.ident[0:N, 0:N])
            last.then_inc(pt_d, 1)
            pe.wait_ge(pt_e, 1)
            pe.wait_ge(ldv, 16 * NS)
            for h in range(NMH):
                for b in range(NS):
                    j = h * NS + b
                    for t in range(2):
                        last = nc.tensor.matmul(b2[:, j:j + 1], vb[:, b, t, h * 128:(h + 1) * 128], pT[:, t, j:j + 1], start=(t == 0), stop=(t == 1))
            last.then_inc(o_d, 1)

        @block.scalar
        def _(act):
            for b in range(NS):
                act.wait_ge(kt_d, b + 1)
                if b >= 2:
                    act.wait_ge(s_d, b - 1)
                for h in range(2):
                    nc.scalar.activation(kt[b % 2][:, 2 * h:2 * h + 2, :], m.bank[2 * (b % 2) + h][:, :].rearrange("p (h k) -> p h k", h=2),
                                         ACT.Copy).then_inc(kt_e, 1)
            act.wait_ge(m_r, 1)
            nc.scalar.activation(pr[:, :], b0[0:N, 0:M], ACT.Exp, bias=st[:, 1:2], scale=MEM_SCALE, accum_out=st[:, 2:3]).then_inc(e_d, 1)

        @block.vector
        def _(v):
            c = Chain(v, ch)
            v.wait_ge(s_d, NS)
            nc.vector.tensor_copy(sT[:, :, :], b4[:, 0:2 * N].rearrange("p (t n) -> p t n", t=2)).then_inc(s_e, 1)
            v.wait_ge(t_d, 1)
            c.link(nc.vector.reduce_max(st[:, 0:1], b0[0:N, 0:M], AX_X))
            nc.vector.tensor_scalar(st[:, 1:2], st[:, 0:1], -MEM_SCALE, None, ALU.mult).then_inc(m_r, 1)
            v.wait_ge(e_d, 1)
            c.link(nc.vector.reciprocal(st[:, 3:4], st[:, 2:3]))
            nc.vector.tensor_scalar(pr[:, :], pr[:, :], st[:, 3:4], None, ALU.mult).then_inc(p_r, 1)
            v.wait_ge(pt_d, 1)
            nc.vector.tensor_copy(pT[:, :, :], b1[:, 0:2 * N].rearrange("p (t n) -> p t n", t=2)).then_inc(pt_e, 1)
            c.link(nc.vector.scalar_tensor_tensor(gz[:, :, :], m.gth_s[:, 0:NMH, :], 1.0, m.gh_s[:, 0:NMH, :], ALU.add, ALU.mult))
            v.wait_ge(o_d, 1)
            nc.vector.tensor_tensor(m.zs[:, 0:NMH, :], gz[:, :, :], b2[:, 0:N].rearrange("p (h s) -> p h s", h=NMH), ALU.mult)


def kv_phase(nc, m, sem, A, outs):
    ldw, tab, st = sem("kv_ldw"), sem("kv_tab"), sem("kv_st")
    whi, wlo, hhi, hlo, mmd, kr, kvv, tr, ev, ch, zz = (sem("kv_" + s) for s in ("whi", "wlo", "hhi", "hlo", "mmd", "kr", "kvv", "tr", "ev", "ch", "zz"))
    H = m.HI
    NK = 256
    raw = m.at("kv_raw", [128, KT, NK], H)
    wl = m.at("kv_wl", [128, KT, NK], H, F32R)
    wh = m.at("kv_wh", [128, KT, NK], H + 8192, F32R)
    hh = [m.at(f"kv_hh{i}", [128, KT, 128], H + 16384 + 4096 * i, F32R) for i in range(2)]
    hl = [m.at(f"kv_hl{i}", [128, KT, 128], H + 24576 + 4096 * i, F32R) for i in range(2)]
    cs = m.at("kv_cs", [128, 2, TT + 1, 32], H + 32768)
    t1 = m.at("kv_t1", [128, 2, 2, 32], H + 32768 + 8704)
    t2 = m.at("kv_t2", [128, 2, 2, 32], H + 32768 + 8704 + 512)
    kn = [m.at(f"kv_kn{i}", [128, 2, 2, 32], H + 32768 + 8704 + 1024 + 512 * i) for i in range(2)]
    vlast = m.kV
    g = lambda k: m.prm[:, k, R_KVG:R_KVG + 1]
    rows = lambda t: 128 if t < TT else NS
    kvb = [m.bank[0], m.bank[1]]
    with nc.Block() as block:
        @block.sync
        def _(s):
            s.dma_start(raw[:, :, :], A["w_kv"].rearrange("(k p) n -> p k n", p=128)).then_inc(ldw, 16)
            s.dma_start(cs[:, :, :, :], A["rope_k"]).then_inc(tab, 16)
            s.dma_start(outs["wk_s"][:, 0:W - 1], A["cache_win_k"][:, 1:W]).then_inc(st, 16)
            s.dma_start(outs["wv_s"][:, 0:W - 1], A["cache_win_v"][:, 1:W]).then_inc(st, 16)
            s.wait_ge(kr, TT)
            s.dma_start(outs["wk_p"][0].rearrange("w g d -> w (g d)"), kn[(TT - 1) % 2][:, :, :, :].rearrange("p g h d -> p (g h d)")).then_inc(st, 16)
            s.wait_ge(kvv, TT)
            s.dma_start(outs["wv_p"][0].rearrange("w g d -> w (g d)"), m.kV[:, TT, :]).then_inc(st, 16)
            s.wait_ge(kvv, TT + 2)
            s.dma_start(outs["wk_s"][:, W - 1].rearrange("b g d -> b (g d)"), m.knew[0:NS, 0:128]).then_inc(st, 16)
            s.dma_start(outs["wv_s"][:, W - 1].rearrange("b g d -> b (g d)"), m.knew[0:NS, 128:256]).then_inc(st, 16)
            s.wait_ge(st, 96)

        @block.gpsimd
        def _(gp):
            gp.memset(m.kT[:, 0:128], 0.0).then_inc(zz, 1)
            gp.memset(m.kV[:, 0, :], 0.0).then_inc(zz, 1)

        @block.scalar
        def _(act):
            act.wait_ge(ldw, 16)
            nc.scalar.activation(wh[:, :, :], raw[:, :, :], ACT.Copy).then_inc(whi, 1)
            for t in range(TT + 1):
                n = rows(t)
                if t >= 2:
                    act.wait_ge(mmd, t - 1)
                for k in range(KT):
                    nc.scalar.activation(hh[t % 2][:, k, 0:n], m.hn[:, k, t * 128:t * 128 + n], ACT.Copy, scale=g(k)).then_inc(hhi, 1)

        @block.vector
        def _(v):
            c = Chain(v, ch)
            v.wait_ge(whi, 1)
            nc.vector.tensor_tensor(wl[:, :, :], raw[:, :, :], wh[:, :, :].bitcast(F32), ALU.subtract).then_inc(wlo, 1)
            v.wait_ge(tab, 16)

            def rope(t):
                n, ps = rows(t), kvb[t % 2]
                v.wait_ge(mmd, t + 1)
                if t:
                    v.wait_ge(kr, t)
                k = ps[0:n, 0:128].rearrange("p (g h d) -> p g h d", g=2, h=2)
                cb, sb = (cs[0:n, j, t, :].unsqueeze(1).broadcast_to([n, 2, 32]) for j in range(2))
                for h in range(2):
                    nc.vector.tensor_tensor(t1[0:n, :, h, :], k[:, :, h, :], cb, ALU.mult)
                    r = nc.vector.tensor_tensor(t2[0:n, :, h, :], k[:, :, 1 - h, :], sb, ALU.mult)
                c.link(r)
                out = kn[t % 2][0:n] if t < TT else m.knew[0:n, 0:128].rearrange("p (g h d) -> p g h d", g=2, h=2)
                if t >= 2:
                    v.wait_ge(tr, t - 1)
                for h, op in ((0, ALU.subtract), (1, ALU.add)):
                    r = nc.vector.tensor_tensor(out[:, :, h, :], t1[0:n, :, h, :], t2[0:n, :, h, :], op)
                if t < TT:
                    r.then_inc(kr, 1)
                else:
                    r.then_inc(kvv, 1)
                nc.vector.tensor_copy(m.kV[:, t + 1, :] if t < TT else m.knew[0:n, 128:256], ps[0:n, 128:256]).then_inc(kvv, 1)

            def evac(t):
                v.wait_ge(tr, t + 1)
                nc.vector.tensor_copy(m.kT[:, (t + 1) * 128:(t + 2) * 128], m.bank[2 + t % 2][:, 0:128]).then_inc(ev, 1)

            for t in range(TT + 1):
                n = rows(t)
                if t >= 2:
                    v.wait_ge(mmd, t - 1)
                for k in range(KT):
                    v.wait_ge(hhi, KT * t + k + 1)
                    r = nc.vector.scalar_tensor_tensor(hl[t % 2][:, k, 0:n], m.hn[:, k, t * 128:t * 128 + n], g(k),
                                                       hh[t % 2][:, k, 0:n].bitcast(F32), ALU.mult, ALU.subtract)
                r.then_inc(hlo, 1)
                if t >= 1:
                    rope(t - 1)
                if t >= 2:
                    evac(t - 2)
            rope(TT)
            evac(TT - 1)

        @block.tensor
        def _(pe):
            pe.wait_ge(wlo, 1)

            def kt_tile(t):
                pe.wait_ge(kr, t + 1)
                if t >= 2:
                    pe.wait_ge(ev, t - 1)
                nc.tensor.transpose(m.bank[2 + t % 2][:, 0:128], kn[t % 2][:, :, :, :].rearrange("p g h d -> p (g h d)"), m.ident[:, :]).then_inc(tr, 1)

            for t in range(TT + 1):
                n = rows(t)
                pe.wait_ge(hlo, t + 1)
                if t >= 2:
                    pe.wait_ge(kvv, t - 1)
                for k in range(KT):
                    a, b = hh[t % 2][:, k, 0:n], hl[t % 2][:, k, 0:n]
                    for q, (s_, r_) in enumerate(((a, wh), (a, wl), (b, wh))):
                        last = nc.tensor.matmul(kvb[t % 2][0:n, 0:NK], s_, r_[:, k, :], start=(k == 0 and q == 0), stop=(k == KT - 1 and q == 2))
                last.then_inc(mmd, 1)
                if t >= 1:
                    kt_tile(t - 1)


def sample_window_phase(nc, m, sem, A):
    ld, sw, kt_d, kt_e, q_r, s_d, s_e, t_d, m_r, e_d, p_r, pt_d, pt_e, o_d, ch, k0 = (sem("sw_" + s) for s in
        "ld sw kt_d kt_e q_r s_d s_e t_d m_r e_d p_r pt_d pt_e o_d ch k0".split())
    H = m.HI
    kw = m.at("sw_k", [128, NS, 128], H)
    vw = m.at("sw_v", [128, NS, 128], H + 4096)
    kt = m.at("sw_kt", [128, NS, 128], H + 8192)
    qr = m.at("sw_qr", [128, KT, NS], H + 12288)
    q1 = m.at("sw_q1", [128, KT, NS], H + 12544)
    qs = m.at("sw_qs", [128, KT, NS], H + 12800)
    cs = m.at("sw_cs", [128, 2], H + 13056)
    sT = m.at("sw_sT", [128, NS, 2, KT], H + 13312)
    pr = m.at("sw_p", [128, 128], H + 13824)
    pT = m.at("sw_pT", [128, 128], H + 14336)
    gz = m.at("sw_gz", [128, KT, NS], H + 14848)
    st = m.at("sw_st", [128, 8], H + 15104)
    u = m.bs[:, NMH:NI, :]
    with nc.Block() as block:
        @block.sync
        def _(s):
            for j, (dst, src) in enumerate(((kw, "cache_win_k"), (vw, "cache_win_v"))):
                s.dma_start(dst[1:128, :, :], A[src][:, 1:W].rearrange("b w g d -> w b (g d)")).then_inc(ld, 16)
                for b in range(NS):
                    s.dma_start(dst[0:1, b, :], m.knew[b:b + 1, j * 128:(j + 1) * 128]).then_inc(ld, 16)
            s.dma_start(cs[:, :], A["rope_q"][:, :, T], allow_slow_non_contiguous=True).then_inc(sw, 16)
            for r in range(4):
                s.dma_start(qr[32 * r:32 * r + 32, :, :], u[32 * (r ^ 1):32 * (r ^ 1) + 32, :, :]).then_inc(sw, 16)

        @block.tensor
        def _(pe):
            pe.wait_ge(ld, 16 * 2 * (NS + 1))
            for b in range(NS):
                last = nc.tensor.transpose(m.bank[b // 4][:, (b % 4) * 128:(b % 4 + 1) * 128], kw[:, b, :], m.ident[:, :])
            last.then_inc(kt_d, 1)
            pe.wait_ge(kt_e, 2)
            pe.wait_ge(q_r, 1)
            for g in range(2):
                for b in range(NS):
                    last = nc.tensor.matmul(m.bank[2 + g][:, b * 8:b * 8 + 8], kt[64 * g:64 * g + 64, b, :], qs[64 * g:64 * g + 64, :, b], start=True, stop=True)
            last.then_inc(s_d, 1)
            pe.wait_ge(s_e, 1)
            nc.tensor.transpose(m.bank[0][:, 0:128], sT[:, :, :, :].rearrange("p b g j -> p (b g j)"), m.ident[:, :]).then_inc(t_d, 1)
            pe.wait_ge(p_r, 1)
            nc.tensor.transpose(m.bank[1][:, 0:128], pr[:, :], m.ident[:, :]).then_inc(pt_d, 1)
            pe.wait_ge(pt_e, 1)
            for g in range(2):
                for b in range(NS):
                    last = nc.tensor.matmul(m.bank[4][64 * g:64 * g + 64, b * 8:b * 8 + 8], vw[:, b, 64 * g:64 * g + 64],
                                            pT[:, b * 16 + g * 8:b * 16 + g * 8 + 8], start=True, stop=True)
            last.then_inc(o_d, 1)

        @block.scalar
        def _(act):
            act.wait_ge(kt_d, 1)
            for h in range(2):
                nc.scalar.activation(kt[:, 4 * h:4 * h + 4, :], m.bank[h][:, :].rearrange("p (b k) -> p b k", b=4), ACT.Copy).then_inc(kt_e, 1)
            act.wait_ge(m_r, 2)
            nc.scalar.activation(st[:, 4:5], m.sink_col[:, :], ACT.Exp, bias=st[:, 2:3])
            nc.scalar.activation(pr[:, :], m.bank[0][:, 0:128], ACT.Exp, bias=st[:, 2:3], accum_out=st[:, 3:4]).then_inc(e_d, 1)

        @block.vector
        def _(v):
            c = Chain(v, ch)
            v.wait_ge(sw, 80)
            c.link(nc.vector.tensor_scalar(q1[:, :, :], qr[:, :, :], cs[:, 1:2], None, ALU.mult))
            nc.vector.scalar_tensor_tensor(qs[:, :, :], u, cs[:, 0:1], q1[:, :, :], ALU.mult, ALU.add).then_inc(q_r, 1)
            v.wait_ge(s_d, 1)
            nc.vector.tensor_copy(sT[:, :, 0, :], m.bank[2][:, 0:64].rearrange("p (b j) -> p b j", b=NS))
            nc.vector.tensor_copy(sT[:, :, 1, :], m.bank[3][:, 0:64].rearrange("p (b j) -> p b j", b=NS)).then_inc(s_e, 1)
            v.wait_ge(t_d, 1)
            c.link(nc.vector.reduce_max(st[:, 0:1], m.bank[0][:, 0:128], AX_X))
            c.link(nc.vector.tensor_tensor(st[:, 1:2], st[:, 0:1], m.sink_col[:, :], ALU.max))
            nc.vector.tensor_scalar(st[:, 2:3], st[:, 1:2], -1.0, None, ALU.mult).then_inc(m_r, 2)
            v.wait_ge(e_d, 1)
            c.link(nc.vector.tensor_tensor(st[:, 5:6], st[:, 3:4], st[:, 4:5], ALU.add))
            c.link(nc.vector.reciprocal(st[:, 6:7], st[:, 5:6]))
            nc.vector.tensor_scalar(pr[:, :], pr[:, :], st[:, 6:7], None, ALU.mult).then_inc(p_r, 1)
            v.wait_ge(pt_d, 1)
            nc.vector.tensor_copy(pT[:, :], m.bank[1][:, 0:128]).then_inc(pt_e, 1)
            c.link(nc.vector.scalar_tensor_tensor(gz[:, :, :], m.gth_s[:, NMH:NI, :], 1.0, m.gh_s[:, NMH:NI, :], ALU.add, ALU.mult))
            v.wait_ge(o_d, 1)
            nc.vector.tensor_tensor(m.zs[:, NMH:NI, :], gz[:, :, :], m.bank[4][:, 0:64].rearrange("p (b j) -> p j b", b=NS), ALU.mult)


def output_phase(nc, m, sem, l, A, outs):
    P = f"op{l}_"
    V0 = m.V0
    stage = [m.at(P + f"st{i}", [128, D], V0 + 4096 * i) for i in range(4)]
    zr = [m.at(P + f"zr{i}", [128, NI, 128], V0 + 6144 * i) for i in range(2)]
    zl = [m.at(P + f"zl{i}", [128, NI, 128], V0 + 6144 * i, F32R) for i in range(2)]
    zh = [m.at(P + f"zh{i}", [128, NI, 128], V0 + 12288 + 6144 * i, F32R) for i in range(2)]
    x = [m.at(P + f"x{i}", [128, D], V0 + 24576 + 4096 * i) for i in range(3)]
    y = [m.at(P + f"y{i}", [128, D], V0 + 36864 + 4096 * i) for i in range(2)]
    fg = m.at(P + "fg", [128, D], V0 + 45056)
    st = m.stat
    ldw = [sem(P + f"ldw{i}") for i in range(4)]
    ldz = [sem(P + f"ldz{i}") for i in range(2)]
    ldx = [sem(P + f"ldx{i}") for i in range(3)]
    sx = [sem(P + f"sx{i}") for i in range(3)]
    whi, wlo, zhi, zlo, mmd, xn, ss, yn, tr, hev, ch, fgl, zsp = (sem(P + s) for s in
        "whi wlo zhi zlo mmd xn ss yn tr hev ch fgl zsp".split())
    rows = lambda t: 128 if t < TT else NS

    def wrows(k):
        if k < NMH:
            return [(D + 128 * k, 128, 0)]
        j = k - NMH
        return [(128 * j, 128, 0)] if l == 0 else [(64 * j, 64, 0), (512 + 64 * j, 64, 64)]

    with nc.Block() as block:
        @block.sync
        def _(s):
            for k in range(NI):
                if k >= 4:
                    s.wait_ge(wlo, k - 3)
                for r0, n, o in wrows(k):
                    s.dma_start(stage[k % 4][o:o + n, :], A["w_out"][l, r0:r0 + n, :]).then_inc(ldw[k % 4], 16)
        
        @block.scalar
        def _(act):
            seen = [0] * 4
            for k in range(NI):
                seen[k % 4] += 16 * len(wrows(k))
                act.wait_ge(ldw[k % 4], seen[k % 4])
                nc.scalar.activation(m.wo_hi[:, k, :], stage[k % 4][:, :], ACT.Copy).then_inc(whi, 1)

        @block.vector
        def _(v):
            for k in range(NI):
                v.wait_ge(whi, k + 1)
                nc.vector.tensor_tensor(m.wo_lo[:, k, :], stage[k % 4][:, :], m.wo_hi[:, k, :].bitcast(F32), ALU.subtract).then_inc(wlo, 1)
            c = Chain(v, zsp)
            nc.vector.tensor_copy(m.zs_hi[:, :, :], m.zs[:, :, :]).then_inc(zsp, 1)
            v.wait_ge(zsp, 1)
            nc.vector.tensor_tensor(m.zs_lo[:, :, :], m.zs[:, :, :], m.zs_hi[:, :, :].bitcast(F32), ALU.subtract)

    xsrc = lambda t: ((A["x_prompt"][0, t * 128:(t + 1) * 128, :] if t < TT else A["x_sample"].rearrange("b s d -> (b s) d")) if l == 0
                      else m.x1_d[t * 128:t * 128 + rows(t), :])
    xdst = lambda t: (m.x1_d[t * 128:t * 128 + rows(t), :] if l == 0
                      else (outs["y_p"][0, t * 128:(t + 1) * 128, :] if t < TT else outs["y_s"].rearrange("b s d -> (b s) d")))
    with nc.Block() as block:
        @block.sync
        def _(s):
            if l == 1:
                s.dma_start(fg[:, :], A["final_g"].unsqueeze(0).broadcast_to([128, D])).then_inc(fgl, 16)

            def load(t):
                if t < TT:
                    if t >= 2:
                        s.wait_ge(mmd, 2 * (t - 1))
                    s.dma_start(zr[t % 2][:, :, :], m.z_d[:, :, t * 128:(t + 1) * 128].rearrange("k p t -> p k t")).then_inc(ldz[t % 2], 16)
                if t >= 3:
                    s.wait_ge(yn, t - 2)
                    if l == 0:
                        s.wait_ge(sx[t % 3], 16 * (t // 3))
                s.dma_start(x[t % 3][0:rows(t), :], xsrc(t)).then_inc(ldx[t % 3], 16)

            load(0)
            load(1)
            for t in range(TT + 1):
                if l == 0:
                    s.wait_ge(xn, 2 * (t + 1))
                    s.dma_start(xdst(t), x[t % 3][0:rows(t), :]).then_inc(sx[t % 3], 16)
                if t + 2 <= TT:
                    load(t + 2)
                if l == 1:
                    s.wait_ge(yn, t + 1)
                    s.dma_start(xdst(t), y[t % 2][0:rows(t), :]).then_inc(sx[t % 2], 16)
            for i in range(3):
                n = len([t for t in range(TT + 1) if t % (3 if l == 0 else 2) == i]) if (l == 0 or i < 2) else 0
                if n:
                    s.wait_ge(sx[i], 16 * n)

        @block.scalar
        def _(act):
            def split(t):
                act.wait_ge(ldz[t % 2], 16 * (t // 2 + 1))
                if t >= 2:
                    act.wait_ge(mmd, 2 * (t - 1))
                nc.scalar.activation(zh[t % 2][:, :, :], zr[t % 2][:, :, :], ACT.Copy).then_inc(zhi, 1)

            split(0)
            for t in range(TT + 2):
                if t + 1 < TT:
                    split(t + 1)
                if l == 0 and t >= 1:
                    u = t - 1
                    act.wait_ge(tr, u + 1)
                    for h in range(2):
                        i = nc.scalar.activation(m.hn[:, 4 * h:4 * h + 4, u * 128:u * 128 + rows(u)],
                                                 m.bank[4 + 2 * (u % 2) + h][:, :].rearrange("p (k c) -> p k c", k=4)[:, :, 0:rows(u)], ACT.Copy)
                    i.then_inc(hev, 1)
                if t <= TT:
                    n, p = rows(t), t % 2
                    act.wait_ge(xn, 2 * (t + 1))
                    if t >= 2:
                        if l == 0:
                            act.wait_ge(tr, t - 1)
                        else:
                            act.wait_ge(sx[p], 16 * (t // 2))
                    nc.scalar.activation(y[p][0:n, :], x[t % 3][0:n, :], ACT.Square, accum_out=st[0:n, p:p + 1]).then_inc(ss, 1)
                    act.wait_ge(ss, 2 * t + 1)
                    nc.scalar.activation(st[0:n, 2 + p:3 + p], st[0:n, p:p + 1], ACT.Sqrt, bias=m.eps[0:n, :], scale=1.0 / D).then_inc(ss, 1)

        @block.vector
        def _(v):
            c = Chain(v, ch)

            def split(t):
                v.wait_ge(zhi, t + 1)
                nc.vector.tensor_tensor(zl[t % 2][:, :, :], zr[t % 2][:, :, :], zh[t % 2][:, :, :].bitcast(F32), ALU.subtract).then_inc(zlo, 1)

            split(0)
            for t in range(TT + 1):
                n, p = rows(t), t % 2
                if t + 1 < TT:
                    split(t + 1)
                v.wait_ge(ldx[t % 3], 16 * (t // 3 + 1))
                for h in range(2):
                    v.wait_ge(mmd, 2 * t + h + 1)
                    xs = x[t % 3][0:n, h * 512:(h + 1) * 512]
                    nc.vector.tensor_tensor(xs, xs, m.bank[2 * p + h][0:n, :], ALU.add).then_inc(xn, 1)
                v.wait_ge(ss, 2 * t + 2)
                v.wait_ge(xn, 2 * t + 2)
                c.link(nc.vector.reciprocal(st[0:n, 4 + p:5 + p], st[0:n, 2 + p:3 + p]))
                if l == 0:
                    nc.vector.tensor_scalar(y[p][0:n, :], x[t % 3][0:n, :], st[0:n, 4 + p:5 + p], None, ALU.mult).then_inc(yn, 1)
                else:
                    if t == 0:
                        v.wait_ge(fgl, 16)
                    nc.vector.scalar_tensor_tensor(y[p][0:n, :], x[t % 3][0:n, :], st[0:n, 4 + p:5 + p], fg[0:n, :], ALU.mult, ALU.mult).then_inc(yn, 1)

        @block.tensor
        def _(pe):
            def flip(u):
                pe.wait_ge(yn, u + 1)
                if u >= 2:
                    pe.wait_ge(hev, u - 1)
                n = rows(u)
                for k in range(KT):
                    last = nc.tensor.transpose(m.bank[4 + 2 * (u % 2) + k // 4][:, (k % 4) * 128:(k % 4) * 128 + n],
                                               y[u % 2][0:n, k * 128:(k + 1) * 128], m.ident[0:n, 0:n])
                last.then_inc(tr, 1)

            for t in range(TT + 1):
                n, p = rows(t), t % 2
                if t < TT:
                    pe.wait_ge(zlo, t + 1)
                if t >= 2:
                    pe.wait_ge(xn, 2 * (t - 1))
                for h in range(2):
                    for k in range(NI):
                        a, b = (zh[p][:, k, :], zl[p][:, k, :]) if t < TT else (m.zs_hi[:, k, :], m.zs_lo[:, k, :])
                        wh, wl = m.wo_hi[:, k, h * 512:(h + 1) * 512], m.wo_lo[:, k, h * 512:(h + 1) * 512]
                        for q, (s_, r_) in enumerate(((a, wh), (a, wl), (b, wh))):
                            last = nc.tensor.matmul(m.bank[2 * p + h][0:n, :], s_, r_, start=(k == 0 and q == 0), stop=(k == NI - 1 and q == 2))
                    last.then_inc(mmd, 1)
                    if l == 0 and h == 0 and t >= 1:
                        flip(t - 1)
            if l == 0:
                flip(TT)


def build(nc, A, outs):
    with ExitStack() as ctx:
        m = Mem(nc, ctx)
        held = []

        def sem(name):
            held.append(nc.alloc_semaphore(name=name))
            return held[-1]

        def recycle():
            nc.clear_and_free_semaphores(held)
            held.clear()
            nc.all_engine_barrier()

        A["mem_v"] = outs["mem_v"]
        setup_phase(nc, m, sem, A)
        memory_phase(nc, m, sem, A, outs)
        input_norm_phase(nc, m, sem, A)
        split_phase(nc, m, sem, 0)
        recycle()
        item_phase(nc, m, sem, 0, A)
        sample_rows_phase(nc, m, sem, 0)
        sample_mem_phase(nc, m, sem, 0, A)
        sample_lru_phase(nc, m, sem, A, outs)
        output_phase(nc, m, sem, 0, A, outs)
        recycle()
        kv_phase(nc, m, sem, A, outs)
        split_phase(nc, m, sem, 1)
        item_phase(nc, m, sem, 1, A)
        sample_rows_phase(nc, m, sem, 1)
        sample_mem_phase(nc, m, sem, 1, A)
        recycle()
        sample_window_phase(nc, m, sem, A)
        output_phase(nc, m, sem, 1, A, outs)


_INS = ["x_prompt", "x_sample", "cache_mem_k", "cache_mem_v", "state_lru_h", "state_conv", "cache_win_k", "cache_win_v",
        "mem_prompt", "norm_g", "w_in", "w_out", "mem_norm_g", "w_mem_kv", "conv_w", "conv_b", "lru_wa", "lru_ba",
        "lru_wx", "lru_bx", "lru_lambda", "kv_norm_g", "w_kv", "sinks", "final_g"]
_OUTS = [("y_p", (1, T, D)), ("y_s", (NS, 1, D)), ("mem_k", (2, 1, M, NMH, 128)), ("mem_v", (2, 1, M, NMH, 128)),
         ("lru_p", (1, 1, D)), ("conv_p", (1, 1, 3, D)), ("wk_p", (1, W, 2, HD)), ("wv_p", (1, W, 2, HD)),
         ("lru_s", (1, NS, D)), ("conv_s", (1, NS, 3, D)), ("wk_s", (NS, W, 2, HD)), ("wv_s", (NS, W, 2, HD))]


def rope_tables():
    half = HD // 2
    inv = (np.float32(10000.0) ** (-np.arange(half, dtype=np.float32) / np.float32(half))).astype(np.float32)
    pos = np.concatenate([np.arange(T), np.full(128, T)]).astype(np.float32)
    ang = pos[:, None] * inv[None, :]
    cos, sin = np.cos(ang), np.sin(ang)
    q = np.empty((128, 2, TA), np.float32)
    for r in range(4):
        q[32 * r:32 * r + 32, 0] = cos[:TA].T
        q[32 * r:32 * r + 32, 1] = sin[:TA].T * (-1.0 if r % 2 == 0 else 1.0)
    q *= np.float32(HD ** -0.5)
    k = np.stack([cos, sin]).reshape(2, TT + 1, 128, half).transpose(2, 0, 1, 3)
    return q, np.ascontiguousarray(k, np.float32)


def kernel(**inputs):
    import concourse.bacc as _bacc
    from concourse.bass_utils import run_bass_kernel_spmd as _run

    nc = _bacc.Bacc("TRN2", target_bir_lowering=False, num_devices=1, dynamic_dma_scratch_size=1024)
    arrays, A = {}, {}
    rq, rk = rope_tables()
    for name, a in [(n, np.ascontiguousarray(inputs[n])) for n in _INS] + [("rope_q", rq), ("rope_k", rk)]:
        arrays[f"in_{name}"] = a
        A[name] = nc.dram_tensor(f"in_{name}", a.shape, mybir.dt.from_np(a.dtype), kind="ExternalInput").ap()
    outs = {n: nc.dram_tensor(f"out_{n}", s, F32, kind="ExternalOutput").ap() for n, s in _OUTS}
    build(nc, A, outs)
    r = _run(nc, [arrays], core_ids=[0])
    return tuple(r.results[0][f"out_{n}"] for n, _ in _OUTS)
```
